# Optimizing a Trainium2 kernel written in Bass

```python
import jax, jax.numpy as jnp
from jax import lax
import numpy as np

D_MODEL = 2048
BATCH = 1
SEQ = 256
DEPTH = 1

A_HEADS = 16
A_HEAD_DIM = 128
A_KV_RANK = 256
IDX_HEADS = 16
IDX_DIM = 64
TOPK_MAX = 256
Q_BLOCK = 128
M_HEADS = 8
M_QK_DIM = 128
M_V_DIM = 256
M_CHUNK = 64
N_GROUPS = 4
EXPERTS_PER_GROUP = 4
N_EXPERTS = N_GROUPS * EXPERTS_PER_GROUP
TOP_K_IN_GROUP = 2
EXPERT_FF = 512
PLE_DIM = 256
LN_EPS = 1e-5
DN_ALPHA = (2 * DEPTH) ** 0.25
DN_BETA = (8 * DEPTH) ** -0.25

_SPLITS = (
    ('a_q', A_HEADS * A_HEAD_DIM),
    ('a_ckv', A_KV_RANK),
    ('i_q', IDX_HEADS * IDX_DIM),
    ('i_k', IDX_DIM),
    ('i_w', IDX_HEADS),
    ('m_q', M_HEADS * M_QK_DIM),
    ('m_k', M_HEADS * M_QK_DIM),
    ('m_v', M_HEADS * M_V_DIM),
    ('m_o', M_HEADS * M_V_DIM),
    ('m_i', M_HEADS),
    ('m_f', M_HEADS),
    ('g_a', D_MODEL),
    ('g_m', D_MODEL),
)
IN_WIDTH = sum(n for _, n in _SPLITS)

kernel_name = 'hybrid_dsa_mlstm_hmoe_deepnorm'

F32 = jnp.float32

def _split_cols(a):
    offs = np.cumsum([n for _, n in _SPLITS])[:-1].tolist()
    return jnp.split(a, offs, axis=-1)

def layer_norm(x, g, b):
    xf = x.astype(F32)
    mu = jnp.mean(xf, -1, keepdims=True)
    var = jnp.mean(jnp.square(xf - mu), -1, keepdims=True)
    return ((xf - mu) * lax.rsqrt(var + LN_EPS) * g.astype(F32) + b.astype(F32)).astype(x.dtype)

def rms_norm(x, g):
    xf = x.astype(F32)
    return (xf * lax.rsqrt(jnp.mean(jnp.square(xf), -1, keepdims=True) + LN_EPS) * g.astype(F32)).astype(x.dtype)

def alibi_slopes(n):
    return jnp.exp2(-8.0 * jnp.arange(1, n + 1, dtype=F32) / n)

def dsa_attention(q, kv, iq, ik, iw):
    B, S = q.shape[0], q.shape[1]
    n_keep = min(TOPK_MAX, S // 4)
    n_blocks = S // Q_BLOCK
    slopes = alibi_slopes(A_HEADS)
    key_pos = jnp.arange(S)
    ikf = ik.astype(F32)

    def block(i):
        t0 = i * Q_BLOCK
        qb = lax.dynamic_slice_in_dim(q, t0, Q_BLOCK, axis=1).astype(F32)
        iqb = lax.dynamic_slice_in_dim(iq, t0, Q_BLOCK, axis=1).astype(F32)
        iwb = lax.dynamic_slice_in_dim(iw, t0, Q_BLOCK, axis=1).astype(F32)
        qpos = t0 + jnp.arange(Q_BLOCK)
        rel = jax.nn.relu(jnp.einsum('bqhd,bsd->bqhs', iqb, ikf) * IDX_DIM ** -0.5)
        score = jnp.einsum('bqh,bqhs->bqs', iwb * IDX_HEADS ** -0.5, rel)
        causal = key_pos[None, :] <= qpos[:, None]
        score = jnp.where(causal[None], score, -jnp.inf)
        _, sel = lax.top_k(score, n_keep)
        kv_sel = jax.vmap(lambda kvb, ib: kvb[ib])(kv, sel).astype(F32)
        k_sel, v_sel = kv_sel[..., :A_HEAD_DIM], kv_sel[..., A_HEAD_DIM:]
        logits = jnp.einsum('bqhd,bqnd->bqhn', qb, k_sel) * A_HEAD_DIM ** -0.5
        dist = (qpos[None, :, None] - sel).astype(F32)
        logits = logits - slopes[None, None, :, None] * dist[:, :, None, :]
        valid = sel <= qpos[None, :, None]
        logits = jnp.where(valid[:, :, None, :], logits, -jnp.inf)
        probs = jax.nn.softmax(logits, axis=-1)
        return jnp.einsum('bqhn,bqnd->bqhd', probs, v_sel).astype(q.dtype)

    out = lax.map(block, jnp.arange(n_blocks))
    return out.transpose(1, 0, 2, 3, 4).reshape(B, S, A_HEADS * A_HEAD_DIM)

def mlstm(q, k, v, i_pre, f_pre):
    B, S, H, dk = q.shape
    dv = v.shape[-1]
    L = M_CHUNK
    nc = S // L

    def chunks(a):
        return a.astype(F32).reshape(B, nc, L, H, -1).transpose(0, 3, 1, 2, 4)

    def gchunks(a):
        return a.astype(F32).reshape(B, nc, L, H).transpose(0, 3, 1, 2)

    qc = chunks(q) * dk ** -0.5
    kc = chunks(k)
    vc = chunks(v)
    li = gchunks(i_pre)
    lf = jax.nn.log_sigmoid(gchunks(f_pre))
    bcum = jnp.cumsum(lf, axis=-1)
    b_last = bcum[..., -1]
    tri = jnp.tril(jnp.ones((L, L), dtype=bool))
    dmat = jnp.where(tri, bcum[..., :, None] - bcum[..., None, :] + li[..., None, :], -jnp.inf)
    w_end = b_last[..., None] - bcum + li
    a_end = jnp.max(w_end, axis=-1)
    kw = kc * jnp.exp(w_end - a_end[..., None])[..., None]

    def step(carry, xs):
        C, n, m = carry
        q_c, kw_c, v_c, a_c, bl_c = xs
        inter_num = jnp.einsum('bhlk,bhkv->bhlv', q_c, C)
        inter_den = jnp.einsum('bhlk,bhk->bhl', q_c, n)
        m_new = jnp.maximum(bl_c + m, a_c)
        decay = jnp.exp(bl_c + m - m_new)
        scale = jnp.exp(a_c - m_new)
        C_new = decay[..., None, None] * C + scale[..., None, None] * jnp.einsum('bhlk,bhlv->bhkv', kw_c, v_c)
        n_new = decay[..., None] * n + scale[..., None] * jnp.sum(kw_c, axis=-2)
        return (C_new, n_new, m_new), (inter_num, inter_den, m)

    init = (jnp.zeros((B, H, dk, dv), F32), jnp.zeros((B, H, dk), F32), jnp.zeros((B, H), F32))
    xs = (jnp.moveaxis(qc, 2, 0), jnp.moveaxis(kw, 2, 0), jnp.moveaxis(vc, 2, 0),
          jnp.moveaxis(a_end, 2, 0), jnp.moveaxis(b_last, 2, 0))
    _, (inter_num, inter_den, m_prev) = lax.scan(step, init, xs)
    inter_num = jnp.moveaxis(inter_num, 0, 2)
    inter_den = jnp.moveaxis(inter_den, 0, 2)
    m_prev = jnp.moveaxis(m_prev, 0, -1)

    inter_log = bcum + m_prev[..., None]
    m_row = jnp.maximum(inter_log, jnp.max(dmat, axis=-1))
    inter_w = jnp.exp(inter_log - m_row)
    intra_w = jnp.exp(dmat - m_row[..., None]) * jnp.einsum('bhcjk,bhcsk->bhcjs', qc, kc)
    num = inter_w[..., None] * inter_num + jnp.einsum('bhcjs,bhcsv->bhcjv', intra_w, vc)
    den = inter_w * inter_den + jnp.sum(intra_w, axis=-1)
    h = num / jnp.maximum(jnp.abs(den), jnp.exp(-m_row))[..., None]
    return h.transpose(0, 2, 3, 1, 4).reshape(B, S, H * dv)

def hier_moe(x, w_grp, b_grp, w_exp, b_exp, w_gate, w_up, w_down):
    B, S, D = x.shape
    xt = x.reshape(-1, D)
    xf = xt.astype(F32)
    grp_prob = jax.nn.softmax(xf @ w_grp.astype(F32) + b_grp.astype(F32), axis=-1)
    g_p, g_idx = lax.top_k(grp_prob, 1)
    exp_logits = (xf @ w_exp.astype(F32) + b_exp.astype(F32)).reshape(-1, N_GROUPS, EXPERTS_PER_GROUP)
    in_grp = jnp.take_along_axis(exp_logits, g_idx[:, :, None], axis=1)[:, 0]
    e_prob = jax.nn.softmax(in_grp, axis=-1)
    e_p, e_idx = lax.top_k(e_prob, TOP_K_IN_GROUP)
    e_p = e_p / jnp.sum(e_p, axis=-1, keepdims=True)
    w_in_grp = jnp.einsum('tk,tke->te', e_p, jax.nn.one_hot(e_idx, EXPERTS_PER_GROUP, dtype=F32))
    combine = (g_p[:, :, None] * jax.nn.one_hot(g_idx[:, 0], N_GROUPS, dtype=F32)[:, :, None]
               * w_in_grp[:, None, :]).reshape(-1, N_EXPERTS)
    hg = jnp.einsum('td,edf->tef', xt, w_gate)
    hu = jnp.einsum('td,edf->tef', xt, w_up)
    h = jax.nn.silu(hg) * hu * combine[:, :, None].astype(hg.dtype)
    return jnp.einsum('tef,efd->td', h, w_down).reshape(B, S, D)

def setup_inputs(seed: int = 0) -> dict:
    key = jax.random.key(seed)
    ks = jax.random.split(key, 24)

    def w(k, shape, fan_in, scale=1.0):
        return jax.random.normal(k, shape, F32) * (scale * fan_in ** -0.5)

    def noise(k, shape, s):
        return jax.random.normal(k, shape, F32) * s

    return {
        'x': jax.random.normal(ks[0], (BATCH, SEQ, D_MODEL), F32),
        'p': jax.random.normal(ks[1], (DEPTH, BATCH, SEQ, PLE_DIM), F32),
        'w_in': w(ks[2], (DEPTH, D_MODEL, IN_WIDTH), D_MODEL),
        'kv_norm': 1.0 + noise(ks[3], (DEPTH, A_KV_RANK), 0.02),
        'w_ukv': w(ks[4], (DEPTH, A_KV_RANK, 2 * A_HEAD_DIM), A_KV_RANK),
        'm_i_bias': noise(ks[5], (DEPTH, M_HEADS), 0.1),
        'm_f_bias': 3.0 + noise(ks[6], (DEPTH, M_HEADS), 0.5),
        'w_proj_a': w(ks[7], (DEPTH, A_HEADS * A_HEAD_DIM, D_MODEL), A_HEADS * A_HEAD_DIM),
        'w_proj_m': w(ks[8], (DEPTH, M_HEADS * M_V_DIM, D_MODEL), M_HEADS * M_V_DIM),
        'w_out': w(ks[9], (DEPTH, D_MODEL, D_MODEL), D_MODEL, DN_BETA),
        'ln1_g': 1.0 + noise(ks[10], (DEPTH, D_MODEL), 0.02),
        'ln1_b': noise(ks[11], (DEPTH, D_MODEL), 0.02),
        'w_grp': w(ks[12], (DEPTH, D_MODEL, N_GROUPS), D_MODEL),
        'b_grp': noise(ks[13], (DEPTH, N_GROUPS), 0.01),
        'w_exp': w(ks[14], (DEPTH, D_MODEL, N_EXPERTS), D_MODEL),
        'b_exp': noise(ks[15], (DEPTH, N_EXPERTS), 0.01),
        'w_gate': w(ks[16], (DEPTH, N_EXPERTS, D_MODEL, EXPERT_FF), D_MODEL),
        'w_up': w(ks[17], (DEPTH, N_EXPERTS, D_MODEL, EXPERT_FF), D_MODEL),
        'w_down': w(ks[18], (DEPTH, N_EXPERTS, EXPERT_FF, D_MODEL), EXPERT_FF, DN_BETA),
        'w_ple': w(ks[19], (DEPTH, PLE_DIM, D_MODEL), PLE_DIM, DN_BETA),
        'w_ple_gate': w(ks[20], (DEPTH, D_MODEL, D_MODEL), D_MODEL),
        'ln2_g': 1.0 + noise(ks[21], (DEPTH, D_MODEL), 0.02),
        'ln2_b': noise(ks[22], (DEPTH, D_MODEL), 0.02),
    }

def reference(x, p, w_in, kv_norm, w_ukv, m_i_bias, m_f_bias, w_proj_a, w_proj_m, w_out, ln1_g, ln1_b,
              w_grp, b_grp, w_exp, b_exp, w_gate, w_up, w_down, w_ple, w_ple_gate, ln2_g, ln2_b):
    B, S, _ = x.shape
    h = x
    for l in range(DEPTH):
        (a_q, a_ckv, i_q, i_k, i_w, m_q, m_k, m_v, m_o, m_i, m_f, g_a, g_m) = _split_cols(h @ w_in[l])
        kv = rms_norm(a_ckv, kv_norm[l]) @ w_ukv[l]
        y_a = dsa_attention(a_q.reshape(B, S, A_HEADS, A_HEAD_DIM), kv,
                            i_q.reshape(B, S, IDX_HEADS, IDX_DIM), i_k, i_w)
        y_m = mlstm(m_q.reshape(B, S, M_HEADS, M_QK_DIM), m_k.reshape(B, S, M_HEADS, M_QK_DIM),
                    m_v.reshape(B, S, M_HEADS, M_V_DIM), m_i + m_i_bias[l], m_f + m_f_bias[l])
        y_m = (y_m * jax.nn.sigmoid(m_o.astype(F32))).astype(h.dtype)
        mix = jax.nn.sigmoid(g_a) * (y_a @ w_proj_a[l]) + jax.nn.sigmoid(g_m) * (y_m @ w_proj_m[l])
        h = layer_norm(DN_ALPHA * h + mix @ w_out[l], ln1_g[l], ln1_b[l])
        ff = hier_moe(h, w_grp[l], b_grp[l], w_exp[l], b_exp[l], w_gate[l], w_up[l], w_down[l])
        ple = (p[l] @ w_ple[l]) * jax.nn.sigmoid(h @ w_ple_gate[l])
        h = layer_norm(DN_ALPHA * h + ff + ple, ln2_g[l], ln2_b[l])
    return h


_drawn_inputs = setup_inputs


def setup_inputs(seed=0):
    import zlib

    import numpy as np

    out = dict(_drawn_inputs(seed))
    spreads = {}
    factors = {'kv_norm': 8.0,
     'b_grp': 26.759,
     'b_exp': 32.25,
     'ln2_g': 7.636,
     'ln2_b': 7.802,
     'm_i_bias': 3.492}
    for name, (base, spread) in spreads.items():
        noise = np.random.default_rng([zlib.crc32(name.encode()), seed]).standard_normal(out[name].shape)
        drawn = base * np.exp(spread * noise) if base else spread * noise
        out[name] = __import__('jax').numpy.asarray(drawn.astype(out[name].dtype))
    for name, factor in factors.items():
        out[name] = (out[name] * factor).astype(out[name].dtype)
    return out
```

```python
from contextlib import ExitStack

import concourse.bass as bass
from concourse import mybir

F32 = mybir.dt.float32
F32R = mybir.dt.float32r
I32 = mybir.dt.int32
ALU = mybir.AluOpType
ACT = mybir.ActivationFunctionType
AX = mybir.AxisListType.X

P = 128
NT = 2
TOK = NT * P
D = 2048
KT = D // P
NC = 512
HEADS, DH = 16, 128
RANK = 256
IH, ID = 16, 64
KEEP = TOK // 4
MH, MQ, MV = 8, 128, 256
GROUPS, EPG, FF = 4, 4, 512
NE = GROUPS * EPG
PLE = 256
EPS = 1e-5
ALPHA = 2.0 ** 0.25
NEG = -1.0e30
PAD = -2.0e38
TAKEN = -3.0e38

C_Q, C_IDX, C_MQ, C_MV, C_MO, C_IF, C_GA = 0, 2048, 3408, 5456, 7504, 9552, 9568
C_GM = C_GA + D
IDX_W = C_MQ - C_IDX
C_END = C_GM + D

T_IDX, T_MQ, T_Q, T_MV, T_MO, T_MIX, T_OUT, T_PLE, T_MOE = 0, 3, 7, 11, 15, 19, 35, 39, 43
T_GROUP = 3 * EPG
T_OVER = T_MOE + GROUPS * T_GROUP
G_X, G_MQ, G_Q, G_YM, G_MIX = 0, 8, 16, 24, 32

SLOT_CREDIT = 4
RING_CREDIT = 8
HALVES = 8


class Link:

    def __init__(self, eng, sem, base=0):
        self.eng, self.sem, self.base, self.n = eng, sem, base, 0

    def __call__(self, ins):
        ins.then_inc(self.sem, 1)
        self.n += 1
        self.eng.wait_ge(self.sem, self.base + self.n)


def build(nc, x, p, w_in, kv_norm, w_ukv, m_i_bias, m_f_bias, w_proj_a, w_proj_m, w_out, ln1_g, ln1_b,
          w_grp, b_grp, w_exp, b_exp, w_gate, w_up, w_down, w_ple, w_ple_gate, ln2_g, ln2_b, out):
    with ExitStack() as ctx:
        ctx.enter_context(nc.allow_non_contiguous_dma(reason="narrow columns and broadcasts"))
        start = (nc.sbuf_base + 63) // 64 * 64

        def at(name, shape, offset, dt=F32):
            return nc.alloc_sbuf_tensor_at(name, [P] + shape, dt, offset=start + offset)

        def sem(name):
            return ctx.enter_context(nc.semaphore(name))

        W32 = at("w_ring", [4, 4, NC], 0)
        WH = at("w_hi", [4, 2, NC], 32768, F32R)
        WL = at("w_lo", [4, 2, NC], 49152, F32R)
        Z0, Z1, Z2, Z3 = 65536, 98304, 131072, 163840
        Z4 = Z3 + 33024
        ZC = Z4 + 8192
        ZS = ZC + 4096
        xTh = at("xT_hi", [KT, TOK], Z0, F32R)
        xTl = at("xT_lo", [KT, TOK], Z0 + 16384, F32R)
        wple = at("wple", [2, D], Z0)
        hTh = at("h1T_hi", [KT, TOK], Z0, F32R)
        hTl = at("h1T_lo", [KT, TOK], Z0 + 16384, F32R)
        ygh = at("yg_hi", [4, NC], Z0, F32R)
        ygl = at("yg_lo", [4, NC], Z0 + 8192, F32R)
        sgm = at("moe_sig", [FF], Z0 + 16384)
        gcs = at("moe_gate", [FF], Z0 + 18432)
        hid = at("moe_hidden", [FF], Z0 + 20480)
        hidTh = at("moe_hiddenT_hi", [2, 4, P], Z0 + 22528, F32R)
        hidTl = at("moe_hiddenT_lo", [2, 4, P], Z0 + 26624, F32R)
        tokm = at("mq_rows", [NT, D], Z1)
        rows = at("gate_rows", [13, TOK], Z1)
        wif = at("wif", [KT, 16], Z1 + 16384)
        wifh = at("wif_hi", [KT, 16], Z1 + 17408, F32R)
        wifl = at("wif_lo", [KT, 16], Z1 + 18432, F32R)
        yaTh = at("yaT_hi", [KT, TOK], Z1, F32R)
        yaTl = at("yaT_lo", [KT, TOK], Z1 + 16384, F32R)
        mixTh = at("mixT_hi", [KT, TOK], Z1, F32R)
        mixTl = at("mixT_lo", [KT, TOK], Z1 + 16384, F32R)
        pp = at("ple_products", [NT, D], Z1)
        xgh = at("xg_hi", [KT, P], Z1, F32R)
        xgl = at("xg_lo", [KT, P], Z1 + 8192, F32R)
        sel = at("sel", [NT, GROUPS + 1, P], Z1 + 16384, F32R)
        selT = at("selT", [GROUPS + 1, TOK], Z1 + 21504, F32R)
        wr = at("w_router", [KT, 20], Z1 + 26624)
        wrh = at("w_router_hi", [KT, 20], Z1 + 27904, F32R)
        wrl = at("w_router_lo", [KT, 20], Z1 + 29184, F32R)
        selg = at("moe_sel", [NT, P], Z1 + 26624, F32R)
        selTg = at("moe_selT", [TOK], Z1 + 27648, F32R)
        cg = at("moe_combine", [EPG], Z1 + 28672)
        cslot = at("combine_slots", [GROUPS + 1, EPG], Z1 + 30464)
        iota = at("iota", [P], Z1 + 30720)
        P1 = at("idx_proj", [NT, 1488], Z2)
        iqT = at("iqT", [8, TOK], Z2 + 11904)
        ikT = at("ikT", [TOK], Z2 + 20096)
        kvn = at("kvn", [NT, RANK], Z2 + 21120)
        kvT = at("kvnT", [2, TOK], Z2 + 23168)
        wukv = at("wukv", [2, 2 * DH], Z2 + 25216)
        kvg = at("kv_norm_rows", [RANK], Z2 + 27264)
        RL = at("relu_scores", [2, NC], Z2 + 28288)
        tokq = at("q_rows", [NT, D], Z2)
        aqT = at("aqT", [HEADS, TOK], Z2 + 16384)
        LG = at("logits", [8, TOK], Z2)
        PT = at("probsT", [2, 8 * P], Z2 + 8192)
        YM = at("ym", [NT, D], Z2 + 16384)
        MIX = at("mix", [NT, D], Z2)
        h1h = at("h1_hi", [NT, KT, P], Z2, F32R)
        h1l = at("h1_lo", [NT, KT, P], Z2 + 16384, F32R)
        XS = at("x_rows", [NT, D], Z3)
        mv = at("mv", [NT, MH, MV + 1], Z3)
        mqT = at("mqT", [MH, TOK], Z3 + 16448)
        mkT = at("mkT", [MH, TOK], Z3 + 24640)
        ymTh = at("ymT_hi", [KT, TOK], Z3, F32R)
        ymTl = at("ymT_lo", [KT, TOK], Z3 + 16384, F32R)
        RES = at("res", [NT, D], Z3 + 16384)
        lng = at("ln_g", [D], Z3)
        lnb = at("ln_b", [D], Z3 + 8192)
        ln2g = at("ln2_g_rows", [D], Z3)
        ln2b = at("ln2_b_rows", [D], Z3 + 8192)
        SC = at("idx_scores", [NT, TOK], Z4)
        MK = at("key_mask", [NT, TOK], Z4 + 2048)
        kT = at("kT", [TOK], Z4 + 4096)
        V = at("v", [NT, DH], Z4 + 5120)
        DI = at("distance", [NT, TOK], Z4 + 6144)
        ex = at("mlstm_exp", [384], Z4 + 3072)
        wt = at("mlstm_wT", [384], Z4 + 4608)
        sg = at("gate_sig", [2, NT, NC], Z4)
        pT = at("pT", [2, TOK], Z4)
        pin = at("p_rows", [NT, PLE], Z4 + 2048)
        psg = at("ple_sig", [NT, NC], Z4 + 4096)
        ident = at("ident", [P], ZC)
        identR = at("ident_r", [P], ZC + 512, F32R)
        ones = at("ones", [P], ZC + 1024)
        upper = at("upper", [P], ZC + 1536)
        CM = at("causalT", [TOK], ZC + 2048)
        negG = at("neg_running_max", [TOK], ZC + 3072)
        small = at("small", [768], ZS)
        cols = [0]

        def tiny(n):
            cols[0] += n
            assert cols[0] <= 768
            return small[:, cols[0] - n:cols[0]]

        iw4, m8, rstd, mhalf, nmr = tiny(32), tiny(8), tiny(2), tiny(2), tiny(2)
        mx, rs, ri = tiny(8), tiny(8), tiny(8)
        ift, bif, ut, en = tiny(32), tiny(16), tiny(16), tiny(16)
        dn, rdn = tiny(2), tiny(2)
        bnst, mv2 = tiny(48), tiny(4)
        brt, lgt, rp = tiny(20), tiny(40), tiny(32)
        tk8, r1, r2, r3, r4 = tiny(8), tiny(32), tiny(32), tiny(32), tiny(16)
        oneh, combw, gp, pos, tot, cum = tiny(8), tiny(8), tiny(4), tiny(4), tiny(4), tiny(8)
        flagf, tslot = tiny(4), tiny(10)
        flag = at("flag", [2], ZS + 3072, I32)

        B = [ctx.enter_context(nc.psum_tensor(f"bank{i}", [P, NC], F32)) for i in range(8)]

        slot_taken = sem("slot_taken")
        landed = [sem(f"w_landed{q}") for q in range(4)]
        hi_ready, lo_ready, slot_free = sem("hi_ready"), sem("lo_ready"), sem("slot_free")
        bank_free = [sem("bank_free0"), sem("bank_free1")]
        tp_ready, tp_hi = sem("tp_ready"), sem("tp_hi")
        tp_free = [sem("tp_free0"), sem("tp_free1")]
        ident_ready, const_ready, identr_ready = sem("ident_ready"), sem("const_ready"), sem("identr_ready")
        x_in, small_in = [sem("x_in0"), sem("x_in1")], sem("small_in")
        dve, act, pool = sem("dve_link"), sem("act_link"), sem("pool_link")
        idx_evac = sem("idx_evac")
        idx_T, idx_Tc = sem("idx_T"), sem("idx_T_copied")
        rms_ss, rms_r, kvn_ready = sem("rms_sumsq"), sem("rms_rstd"), sem("kvn_ready")
        kv_T, kv_Tc, kv_mm, kv_c = sem("kv_T"), sem("kv_T_copied"), sem("kv_mm"), sem("kv_copied")
        sc_mm, sc_relu, sc_used = sem("sc_mm"), sem("sc_relu"), sem("sc_used")
        sc_masked, topk_done, mask_ready = sem("sc_masked"), sem("topk_done"), sem("mask_ready")
        lg_bias, lg_mm, lg_read, lg_max, lg_exp = sem("lg_bias"), sem("lg_mm"), sem("lg_read"), sem("lg_max"), sem("lg_exp")
        pr_norm, pt_T, pt_c, pv_mm, pv_hi, pv_lo = (sem("pr_norm"), sem("pt_T"), sem("pt_copied"), sem("pv_mm"),
                                                    sem("pv_hi"), sem("pv_lo"))
        if_in, if_hi, if_lo, if_mm, if_tok, if_T, if_row = (sem("if_in"), sem("if_hi"), sem("if_lo"), sem("if_mm"),
                                                            sem("if_tok"), sem("if_T"), sem("if_row"))
        row_act, row_dve, row_T, row_Tc = sem("row_act"), sem("row_dve"), sem("row_T"), sem("row_T_copied")
        ml_qk, ml_x, ml_exp, ml_w, ml_num, ml_out = (sem("ml_qk"), sem("ml_x"), sem("ml_exp"), sem("ml_w"),
                                                     sem("ml_num"), sem("ml_out"))
        mix_a, mix_ready = sem("mix_a"), sem("mix_ready")
        x2_in, ln_in, res_ready, var_ready, rstd_ready = (sem("x2_in"), sem("ln_in"), sem("res_ready"),
                                                          sem("var_ready"), sem("rstd_ready"))
        nrm_a, nrm_g, nrm_b = sem("norm_scaled"), sem("norm_gained"), sem("norm_biased")
        h1_hi, h1_lo, h1_scaled = sem("h1_hi"), sem("h1_lo"), sem("h1_scaled")
        hT_mm, hT_mml, hT_hi, hT_lo, nmr_ready = sem("hT_mm"), sem("hT_mml"), sem("hT_hi"), sem("hT_lo"), sem("nmr_ready")
        ple_in, pT_mm, pT_c, pp_mm, pp_c, ple_done = (sem("ple_in"), sem("pT_mm"), sem("pT_copied"), sem("pp_mm"),
                                                      sem("pp_copied"), sem("ple_done"))
        r_in, r_hi, r_lo, r_mm, r_exp, r_log = (sem("r_in"), sem("r_hi"), sem("r_lo"), sem("r_mm"), sem("r_exp"), sem("r_log"))
        r_one, r_cum, r_sel, r_selT, r_selTc, r_cs, r_all = (sem("r_one"), sem("r_cum"), sem("r_sel"), sem("r_selT"),
                                                             sem("r_selTc"), sem("r_cs"), sem("r_all"))
        iota_ready = sem("iota_ready")
        selg_ready, g_table = sem("selg_ready"), sem("g_table")
        g_mm, g_hi, g_lo = sem("g_mm"), sem("g_hi"), sem("g_lo")
        e_sig, e_hid, e_T, e_Thi, e_Tlo = sem("e_sig"), sem("e_hid"), sem("e_T"), sem("e_Thi"), sem("e_Tlo")
        y_hi, y_lo, y_mm, y_add, e_link = sem("y_hi"), sem("y_lo"), sem("y_mm"), sem("y_add"), sem("e_link")
        ln2_in, out_done = sem("ln2_in"), sem("out_done")

        def cols_of(w, c0, width=NC):
            v = w.rearrange("(t p) n -> p t n", p=P)
            return lambda q: v[:, 4 * q:4 * q + 4, bass.ds(c0, width)]

        block = ctx.enter_context(nc.Block())

        @block.sync
        def _(sp):
            def load_tile(t, chunk, width=NC):
                for q in range(4):
                    sp.wait_ge(lo_ready, HALVES * t + 2 * q + 2)
                    sp.sem_inc(slot_taken, 1)
                    sp.dma_start(W32[:, q, :, 0:width], chunk(q)).then_inc(landed[q], 16)

            def load_tiles(t0, n, w, c0):
                with sp.Fori(0, n) as i:
                    load_tile(t0 + i, cols_of(w, c0 + NC * i))

            def load_group(t0, g):
                def full(w, e):
                    v = w.rearrange("l e (p t) f -> p (l e) t f", p=P)
                    return lambda q: v[:, bass.ds(EPG * g + e, 1), 4 * q:4 * q + 4, :].rearrange("p e t f -> p (e t) f")

                def down(e):
                    v = w_down.rearrange("l e (t p) (c n) -> p (l e) t c n", p=P, n=NC)
                    return lambda q: v[:, bass.ds(EPG * g + e, 1), :, q, :].rearrange("p e t n -> p (e t) n")

                order = []
                for e in range(EPG):
                    order += [full(w_gate, e), full(w_up, e)]
                    if e:
                        order.append(down(e - 1))
                order.append(down(EPG - 1))
                for k, chunk in enumerate(order):
                    load_tile(t0 + k, chunk)

            for a in range(NT):
                sp.dma_start(XS[:, a, :], x[0, a * P:a * P + P, :]).then_inc(x_in[a], 16)
            for j in range(2):
                load_tile(T_IDX + j, cols_of(w_in[0], C_IDX + NC * j))
            load_tile(T_IDX + 2, cols_of(w_in[0], C_IDX + 2 * NC, IDX_W - 2 * NC), IDX_W - 2 * NC)
            load_tiles(T_MQ, 4, w_in[0], C_MQ)
            load_tiles(T_Q, 4, w_in[0], C_Q)
            load_tiles(T_MV, 8, w_in[0], C_MV)
            with sp.Fori(0, 4) as i:
                load_tile(T_MIX + 4 * i, cols_of(w_in[0], C_GA + NC * i))
                load_tile(T_MIX + 4 * i + 1, cols_of(w_proj_a[0], NC * i))
                load_tile(T_MIX + 4 * i + 2, cols_of(w_in[0], C_GM + NC * i))
                load_tile(T_MIX + 4 * i + 3, cols_of(w_proj_m[0], NC * i))
            load_tiles(T_OUT, 4, w_out[0], 0)
            v = w_ple_gate[0].rearrange("(p t) n -> p t n", p=P)
            with sp.Fori(0, 4) as i:
                load_tile(T_PLE + i, lambda q: v[:, 4 * q:4 * q + 4, bass.ds(NC * i, NC)])
            with sp.Fori(0, GROUPS) as g:
                load_group(T_MOE + T_GROUP * g, g)
            sp.wait_ge(r_all, 1)
            over = sp.value_load(flag[0:1, 0:1], min_val=0, max_val=1)
            group = sp.value_load(flag[0:1, 1:2], min_val=0, max_val=GROUPS - 1)
            with sp.If(over > 0):
                load_group(T_OVER, group)
            for n in range(8):
                a, c = n // 4, n % 4
                sp.wait_ge(nrm_b, 8 + n + 1)
                sp.dma_start(out[0, a * P:a * P + P, c * NC:c * NC + NC], RES[:, a, c * NC:c * NC + NC]).then_inc(out_done, 16)
            sp.wait_ge(out_done, 16 * 8)

        @block.gpsimd
        def _(pl):
            link = Link(pl, pool)
            g = nc.gpsimd

            def tri(t, op, base, pattern, cm, fill):
                link(g.affine_select(out=t, in_=t, compare_op=op, fill=fill, base=base, pattern=pattern,
                                     channel_multiplier=cm))

            link(g.memset(ident[:], 0.0))
            g.affine_select(out=ident[:], in_=ident[:], compare_op=ALU.not_equal, fill=1.0, base=0,
                            pattern=[[-1, P]], channel_multiplier=1).then_inc(ident_ready, 1)
            link(g.memset(ones[:], 1.0))
            link(g.memset(upper[:], 1.0))
            tri(upper[:], ALU.is_ge, 0, [[1, P]], -1, 0.0)
            link(g.memset(CM[:], 0.0))
            tri(CM[:, 0:P], ALU.is_ge, 0, [[1, P]], -1, NEG)
            link(g.memset(mhalf, -0.5))
            g.iota(DI[:], pattern=[[-P, NT], [1, TOK]], base=0, channel_multiplier=-1,
                   allow_small_or_imprecise_dtypes=True).then_inc(const_ready, 1)

            pl.wait_ge(rms_ss, 1)
            g.tensor_tensor(rstd, rstd, mhalf, ALU.pow).then_inc(rms_r, 1)
            pl.wait_ge(sc_used, 2 * IH)
            for a in range(NT):
                w = P * (a + 1)
                g.affine_select(out=SC[:, a, 0:w], in_=SC[:, a, 0:w], compare_op=ALU.is_ge, fill=NEG, base=a * P,
                                pattern=[[-1, w]], channel_multiplier=1).then_inc(sc_masked, 1)
            pl.wait_ge(topk_done, 1)
            for a in range(NT):
                w = P * (a + 1)
                link(g.affine_select(out=MK[:, a, 0:w], in_=MK[:, a, 0:w], compare_op=ALU.is_ge, fill=NEG, base=a * P,
                                     pattern=[[-1, w]], channel_multiplier=1))
            pl.wait_ge(tp_free[0], G_YM // 2)
            pl.wait_ge(tp_free[1], G_YM // 2)
            for b in range(4):
                a, hh = b // 2, b % 2
                w = P * (a + 1)
                if b:
                    pl.wait_ge(pt_T, (2, 4, 8)[b - 1])
                for j in range(8):
                    last = g.tensor_scalar(LG[:, j, 0:w], DI[:, a, 0:w], 2.0 ** (-8.0 * (8 * hh + j + 1) / HEADS), None,
                                           ALU.mult)
                link(last)
                g.tensor_tensor(LG[:, :, 0:w], LG[:, :, 0:w], MK[:, a, 0:w].unsqueeze(1).to_broadcast([P, 8, w]),
                                ALU.add).then_inc(lg_bias, 1)

            def norm(n, ready, br):
                pl.wait_ge(var_ready, n)
                g.tensor_tensor(rstd, rstd, mhalf, ALU.pow).then_inc(rstd_ready, 1)
                for k in range(8):
                    a, c = k // 4, slice(k % 4 * NC, k % 4 * NC + NC)
                    pl.wait_ge(nrm_g, 8 * (n - 1) + k + 1)
                    g.tensor_tensor(RES[:, a, c], RES[:, a, c], br[:, c], ALU.add).then_inc(nrm_b, 1)

            norm(1, ln_in, lnb)
            g.iota(iota[:], pattern=[[1, P]], base=0, channel_multiplier=0,
                   allow_small_or_imprecise_dtypes=True).then_inc(iota_ready, 1)
            for a in range(NT):
                pl.wait_ge(h1_hi, a + 1)
                pl.wait_ge(h1_lo, a + 1)
                g.tensor_scalar(RES[:, a, :], RES[:, a, :], ALPHA, None, ALU.mult).then_inc(h1_scaled, 1)

            def selection(j):
                g.tensor_copy(selg[:], sel[:, :, bass.ds(j, 1), :].bitcast(F32)).then_inc(selg_ready, 1)

            def tables(j):
                pl.wait_ge(y_add, 8 * j + 8)
                g.tensor_copy(selTg[:], selT[:, bass.ds(j, 1), :].bitcast(F32)).then_inc(g_table, 1)
                g.tensor_copy(cg[:], cslot[:, bass.ds(j, 1), :]).then_inc(g_table, 1)

            pl.wait_ge(r_all, 1)
            selection(0)
            with pl.Fori(0, GROUPS) as i:
                tables(i)
                pl.wait_ge(g_mm, 8 * i + 8)
                selection(i + 1)
            over = pl.value_load(flag[0:1, 0:1], min_val=0, max_val=1)
            with pl.If(over > 0):
                tables(GROUPS)
            norm(2, ln2_in, ln2b)

        @block.tensor
        def _(pe):
            mm = nc.tensor.matmul

            def half(t, h, lh, ll, banks, ks, width, start, stop):
                s = h % 4
                pe.wait_ge(hi_ready, HALVES * t + h + 1)
                for kk, k in enumerate(ks):
                    for m, b in enumerate(banks):
                        mm(b, lh(k, m), WH[:, s, kk, 0:width], start=start and kk == 0, stop=False)
                        mm(b, ll(k, m), WH[:, s, kk, 0:width], start=False, stop=False)
                pe.wait_ge(lo_ready, RING_CREDIT + HALVES * t + h + 1)
                for kk, k in enumerate(ks):
                    for m, b in enumerate(banks):
                        last = mm(b, lh(k, m), WL[:, s, kk, 0:width], start=False, stop=stop and kk == 1)
                last.then_inc(slot_free, 1)

            def dense(tb, oh, ol, width=NC, i=0, step=2, after=None):
                s = tb % 2
                pe.wait_ge(bank_free[s], tb // 2 + (step // 2) * i + 1)
                banks = [B[2 * s][:, 0:width], B[2 * s + 1][:, 0:width]]
                for h in range(HALVES):
                    half(tb + step * i, h, lambda k, m: oh[:, k, m * P:m * P + P], lambda k, m: ol[:, k, m * P:m * P + P],
                         banks, (2 * h, 2 * h + 1), width, h == 0, h == HALVES - 1)
                    if after:
                        after(h)

            def turn(g0, src, r):
                a, k4 = r // 4, r % 4
                if g0 + r >= 2:
                    pe.wait_ge(tp_free[r % 2], (g0 + r) // 2)
                for k in range(4):
                    c = (4 * k4 + k) * P
                    last = nc.tensor.transpose(B[4 + r % 2][:, k * P:k * P + P], src[:, a, c:c + P], ident[:])
                last.then_inc(tp_ready, 1)

            def turned(g0):
                pe.wait_ge(tp_free[0], g0 // 2)
                pe.wait_ge(tp_free[1], g0 // 2)

            pe.sem_inc(slot_free, SLOT_CREDIT)
            pe.sem_inc(bank_free[0], 1)
            pe.sem_inc(bank_free[1], 1)
            pe.wait_ge(ident_ready, 1)
            for r in range(8):
                pe.wait_ge(x_in[r // 4], 16)
                turn(G_X, XS, r)
            turned(G_MQ)
            dense(T_IDX, xTh, xTl)
            dense(T_IDX + 1, xTh, xTl)
            dense(T_IDX + 2, xTh, xTl, IDX_W - 2 * NC)

            def idx_turn(n):
                if n == 0:
                    pe.wait_ge(idx_evac, 3)
                if 2 <= n < 4:
                    pe.wait_ge(idx_Tc, n - 1)
                if n < 4:
                    a, r = n // 2, n % 2
                    for k in range(4):
                        c = RANK + (4 * r + k) * P
                        last = nc.tensor.transpose(B[4 + r][:, k * P:k * P + P], P1[:, a, c:c + P], ident[:])
                else:
                    for a in range(NT):
                        last = nc.tensor.transpose(B[6][:, a * P:a * P + P], P1[:, a, 1360:1488], ident[:])
                last.then_inc(idx_T, 1)

            def latent_turn():
                pe.wait_ge(kvn_ready, 1)
                for k in range(2):
                    for a in range(NT):
                        last = nc.tensor.transpose(B[7][:, (2 * k + a) * P:(2 * k + a + 1) * P],
                                                   kvn[:, a, k * P:k * P + P], ident[:])
                last.then_inc(kv_T, 1)

            def keys_values():
                pe.wait_ge(kv_Tc, 1)
                pe.wait_ge(idx_Tc, 5)
                for k in range(2):
                    mm(B[6][:, 0:TOK], wukv[:, k, 0:DH], kvT[:, k, :], start=k == 0, stop=k == 1)
                for a in range(NT):
                    for k in range(2):
                        last = mm(B[7][:, a * P:a * P + P], kvT[:, k, a * P:a * P + P], wukv[:, k, DH:2 * DH],
                                  start=k == 0, stop=k == 1)
                last.then_inc(kv_mm, 1)

            def score_pair(n):
                a, j, w = n // 8, n % 8, P * (n // 8 + 1)
                if n == 0:
                    pe.wait_ge(kv_c, 2)
                if n >= 2:
                    pe.wait_ge(sc_relu, n - 1)
                for r in range(2):
                    hs = slice(64 * r, 64 * r + 64)
                    last = mm(B[4 + 2 * (n % 2) + r][:, 0:w], iqT[hs, j, a * P:a * P + P], ikT[hs, 0:w],
                              start=True, stop=True)
                last.then_inc(sc_mm, 1)

            dense(T_MQ, xTh, xTl, after=lambda h: idx_turn(h - 4) if h >= 4 else None)

            def after(h):
                if h == 0:
                    idx_turn(4)
                    latent_turn()
                if h == 2:
                    keys_values()
                if h >= 4:
                    score_pair(h - 4)
            dense(T_MQ + 1, xTh, xTl, after=after)
            dense(T_MQ + 2, xTh, xTl, after=lambda h: score_pair(4 + h))
            dense(T_MQ + 3, xTh, xTl, after=lambda h: score_pair(12 + h) if h < 4 else None)
            dense(T_Q, xTh, xTl)

            def after(h):
                if h == 0:
                    pe.wait_ge(bank_free[0], (T_Q - 1) // 2 + 2)
                    pe.wait_ge(sc_relu, 16)
                turn(G_MQ, tokm, h)
            dense(T_Q + 1, xTh, xTl, after=after)

            def gate_products(a):
                if a == 0:
                    pe.wait_ge(if_lo, 1)
                ta = slice(a * P, a * P + P)
                for k in range(KT):
                    mm(B[6][:, 16 * a:16 * a + 16], xTh[:, k, ta], wifh[:, k, :], start=k == 0, stop=False)
                    mm(B[6][:, 16 * a:16 * a + 16], xTl[:, k, ta], wifh[:, k, :], start=False, stop=False)
                    last = mm(B[6][:, 16 * a:16 * a + 16], xTh[:, k, ta], wifl[:, k, :], start=False, stop=k == KT - 1)
                last.then_inc(if_mm, 1)

            def after(h):
                if h < 2:
                    gate_products(h)
                if h == 4:
                    pe.wait_ge(if_tok, 1)
                    for gate in range(2):
                        for a in range(NT):
                            last = nc.tensor.transpose(B[7][0:MH, gate * TOK + a * P:gate * TOK + a * P + P],
                                                       ift[:, 16 * a + 8 * gate:16 * a + 8 * gate + 8], ident[:])
                    last.then_inc(if_T, 1)
            dense(T_Q + 2, xTh, xTl, after=after)

            def after(h):
                if h == 6:
                    pe.wait_ge(row_dve, 4)
                    for a in range(NT):
                        nc.tensor.transpose(B[6][:, 8 * a:8 * a + 8], rows[0:MH, 7, a * P:a * P + P], ident[0:MH, 0:MH])
                        last = nc.tensor.transpose(B[6][:, 16 + 8 * a:24 + 8 * a], rows[0:MH, 11, a * P:a * P + P],
                                                   ident[0:MH, 0:MH])
                    last.then_inc(row_T, 1)
            dense(T_Q + 3, xTh, xTl, after=after)
            dense(T_MV, xTh, xTl)

            def after(h):
                if h == 0:
                    pe.wait_ge(bank_free[0], (T_MV - 1) // 2 + 2)
                turn(G_Q, tokq, h)
            dense(T_MV + 1, xTh, xTl, after=after)

            def logits(b, j):
                a, hh, n = b // 2, b % 2, 4 * b + j
                w = P * (a + 1)
                if n == 0:
                    turned(G_YM)
                if n >= 2:
                    pe.wait_ge(lg_read, n - 1)
                for r in range(2):
                    last = mm(B[4 + n % 2][:, r * w:r * w + w], aqT[:, 8 * hh + 2 * j + r, a * P:a * P + P],
                              kT[:, 0:w], start=True, stop=True)
                last.then_inc(lg_mm, 1)

            def probs_turn(b, st):
                ev = (0, 2, 4, 8)[b] + 2 * st
                pe.wait_ge(pr_norm, b + 1)
                if b and st == 0:
                    pe.wait_ge(pv_lo, 2 * b)
                if b == 0:
                    pe.wait_ge(row_Tc, 1)
                for q4 in range(2):
                    if ev + q4 >= 2:
                        pe.wait_ge(pt_c, ev + q4 - 1)
                    for k in range(4):
                        last = nc.tensor.transpose(B[6 + q4][:, k * P:k * P + P],
                                                   LG[:, 4 * q4 + k, st * P:st * P + P], ident[:])
                    last.then_inc(pt_T, 1)

            def values(b, q4):
                a = b // 2
                pe.wait_ge(pt_c, (2, 4, 8, 12)[b])
                for st in range(a + 1):
                    last = mm(B[6 + q4][:, :], V[:, st, :], PT[:, st, q4 * NC:q4 * NC + NC], start=st == 0, stop=st == a)
                last.then_inc(pv_mm, 1)

            def attend(b):
                def after(h):
                    if h < 2:
                        logits(b, 2 * h)
                        logits(b, 2 * h + 1)
                    if h == 4:
                        probs_turn(b, 0)
                    if h == 5 and b >= 2:
                        probs_turn(b, 1)
                    if h >= 6:
                        values(b, h - 6)
                return after

            dense(T_MV + 2, xTh, xTl, after=attend(0))
            dense(T_MV + 3, xTh, xTl, after=attend(1))
            dense(T_MO, xTh, xTl, after=attend(2))
            dense(T_MO + 1, xTh, xTl, after=attend(3))

            def head_scores(h):
                if h:
                    pe.wait_ge(ml_w, h)
                else:
                    pe.wait_ge(bank_free[0], T_MO // 2 + 2)
                    pe.wait_ge(lg_read, 16)
                mm(B[4][:, 0:TOK], ident[0:MH, h:h + 1].to_broadcast([MH, P]), negG[0:MH, :], start=True, stop=True)
                mm(B[5][:, 0:TOK], mkT[:, h, 0:P], mqT[:, h, :], start=True, stop=True)
                mm(B[5][:, TOK:TOK + P], mkT[:, h, P:TOK], mqT[:, h, P:TOK], start=True, stop=True).then_inc(ml_qk, 1)

            def head_values(h):
                pe.wait_ge(ml_w, h + 1)
                if h:
                    pe.wait_ge(ml_out, h)
                else:
                    pe.wait_ge(pv_lo, 8)
                mm(B[6][:, 0:MV + 1], wt[:, 0:P], mv[:, 0, h, :], start=True, stop=True)
                mm(B[7][:, 0:MV + 1], wt[:, P:TOK], mv[:, 0, h, :], start=True, stop=False)
                mm(B[7][:, 0:MV + 1], wt[:, TOK:384], mv[:, 1, h, :], start=False, stop=True).then_inc(ml_num, 1)

            def recurrent(first):
                def after(h):
                    n = first + h
                    if n >= 3 and (n - 3) % 2 == 0 and (n - 3) // 2 < MH:
                        head_values((n - 3) // 2)
                    if n >= 0 and n % 2 == 0 and n // 2 < MH:
                        head_scores(n // 2)
                return after
            dense(T_MO + 2, xTh, xTl, after=recurrent(-2))
            dense(T_MO + 3, xTh, xTl, after=recurrent(6))
            dense(T_MIX, xTh, xTl, after=recurrent(14))
            dense(T_MIX + 1, yaTh, yaTl)

            def after(h):
                if h == 0:
                    pe.wait_ge(ml_out, MH)
                turn(G_YM, YM, h)
            dense(T_MIX + 2, xTh, xTl, after=after)
            turned(G_MIX)
            dense(T_MIX + 3, ymTh, ymTl)
            with pe.Fori(1, 3) as i:
                dense(T_MIX, xTh, xTl, i=i, step=4)
                dense(T_MIX + 1, yaTh, yaTl, i=i, step=4)
                dense(T_MIX + 2, xTh, xTl, i=i, step=4)
                dense(T_MIX + 3, ymTh, ymTl, i=i, step=4)
            dense(T_MIX + 12, xTh, xTl)
            dense(T_MIX + 13, yaTh, yaTl)
            dense(T_MIX + 14, xTh, xTl)

            order = (0, 4, 1, 5, 2, 6, 3, 7)

            def mix_turn(n):
                r = order[n]
                if n >= 1:
                    pe.wait_ge(tp_free[n % 2], (G_MIX + n) // 2)
                a, k4 = r // 4, r % 4
                pe.wait_ge(mix_ready, k4 + 1)
                for k in range(4):
                    c = (4 * k4 + k) * P
                    last = nc.tensor.transpose(B[4 + n % 2][:, k * P:k * P + P], MIX[:, a, c:c + P], ident[:])
                last.then_inc(tp_ready, 1)

            dense(T_MIX + 15, ymTh, ymTl, after=lambda h: mix_turn(h - 1) if 1 <= h < 7 else None)

            def after(h):
                if h in (3, 4):
                    mix_turn(h + 3)
                if h == 5:
                    turned(G_MIX + 8)
            turned(G_MIX + 6)
            dense(T_OUT, mixTh, mixTl, after=after)
            dense(T_OUT + 1, mixTh, mixTl)
            dense(T_OUT + 2, mixTh, mixTl)

            def after(h):
                if h == 0:
                    pe.wait_ge(ple_in, 32)
                    for k in range(2):
                        for a in range(NT):
                            last = nc.tensor.transpose(B[6][:, (2 * k + a) * P:(2 * k + a + 1) * P],
                                                       pin[:, a, k * P:k * P + P], ident[:])
                    last.then_inc(pT_mm, 1)
            dense(T_OUT + 3, mixTh, mixTl, after=after)
            pe.wait_ge(pT_c, 1)
            for n in range(8):
                a, c = n // 4, n % 4
                if n >= 4:
                    pe.wait_ge(pp_c, n - 3)
                for k in range(2):
                    last = mm(B[4 + n % 4][:, :], pT[:, k, a * P:a * P + P], wple[:, k, c * NC:c * NC + NC],
                              start=k == 0, stop=k == 1)
                last.then_inc(pp_mm, 1)

            pe.wait_ge(identr_ready, 1)
            pe.wait_ge(pp_c, 8)
            for a in range(NT):
                for src, ready, read, b in ((h1h, h1_hi, hT_hi, 4), (h1l, h1_lo, hT_lo, 6)):
                    pe.wait_ge(ready, a + 1)
                    for k4 in range(4):
                        n = 4 * a + k4
                        if n >= 2:
                            pe.wait_ge(read, n - 1)
                        for k in range(4):
                            last = mm(B[b + n % 2][:, k * P:k * P + P], src[:, a, 4 * k4 + k, :], identR[:],
                                      start=True, stop=True)
                        last.then_inc(hT_mm if b == 4 else hT_mml, 1)
            pe.wait_ge(hT_hi, 8)
            pe.wait_ge(hT_lo, 8)

            def router(a):
                pe.wait_ge(r_lo, 1)
                ta = slice(a * P, a * P + P)
                for k in range(KT):
                    o = B[7][:, 20 * a:20 * a + 20]
                    mm(o, hTh[:, k, ta], wrh[:, k, :], start=k == 0, stop=False)
                    mm(o, hTl[:, k, ta], wrh[:, k, :], start=False, stop=False)
                    last = mm(o, hTh[:, k, ta], wrl[:, k, :], start=False, stop=k == KT - 1)
                last.then_inc(r_mm, 1)

            dense(T_PLE, hTh, hTl, after=lambda h: router(h) if h < 2 else None)

            def after(h):
                if h == 4:
                    pe.wait_ge(r_one, 1)
                    mm(B[6][:, 0:4], upper[:], oneh[:, 0:4], start=True, stop=True)
                    mm(B[6][:, 4:8], ones[:], oneh[:, 0:4], start=True, stop=False)
                    mm(B[6][:, 4:8], upper[:], oneh[:, 4:8], start=False, stop=True)
                    mm(B[6][:, 8:12], ones[:], oneh[:, 0:4], start=True, stop=False)
                    mm(B[6][:, 8:12], ones[:], oneh[:, 4:8], start=False, stop=True).then_inc(r_cum, 1)
            dense(T_PLE + 1, hTh, hTl, after=after)

            def slots_turn(j):
                if j == 0:
                    pe.wait_ge(r_sel, 1)
                if j >= 2:
                    pe.wait_ge(r_selTc, j - 1)
                for a in range(NT):
                    last = mm(B[4 + j % 2][:, a * P:a * P + P], sel[:, a, j, :], identR[:], start=True, stop=True)
                last.then_inc(r_selT, 1)

            def slot_weights():
                pe.wait_ge(r_selTc, 1)
                for j in range(GROUPS + 1):
                    for a in range(NT):
                        last = mm(B[6][:, 4 * j:4 * j + 4], sel[:, a, j, :].bitcast(F32), combw[:, 4 * a:4 * a + 4],
                                  start=a == 0, stop=a == 1)
                last.then_inc(r_cs, 1)

            dense(T_PLE + 2, hTh, hTl, after=lambda h: slots_turn(h - 6) if h >= 6 else None)

            def after(h):
                if h < 3:
                    slots_turn(h + 2)
                if h == 3:
                    slot_weights()
            dense(T_PLE + 3, hTh, hTl, after=after)
            pe.wait_ge(bank_free[0], (T_MOE + 1) // 2 + 1)
            pe.wait_ge(bank_free[1], T_MOE // 2 + 1)

            def gather(j, n):
                if n == 0:
                    pe.wait_ge(selg_ready, j + 1)
                if n >= 2:
                    pe.wait_ge(g_hi if n - 2 < 4 else g_lo, 4 * j + (n - 1 if n - 2 < 4 else n - 5))
                src = h1h if n < 4 else h1l
                for k in range(4):
                    for a in range(NT):
                        last = mm(B[n % 2][:, k * P:k * P + P], src[:, a, 4 * (n % 4) + k, :], selg[:, a, :],
                                  start=a == 0, stop=a == 1)
                last.then_inc(g_mm, 1)

            def expert_up(t, j, e):
                for w in range(2):
                    for h in range(HALVES):
                        half(t + w, h, lambda k, m: xgh[:, k, :], lambda k, m: xgl[:, k, :],
                             [B[2 * (e % 2) + w][:, :]], (2 * h, 2 * h + 1), NC, h == 0, h == HALVES - 1)
                    if w == 0 and e:
                        hidden_turn(j, e - 1)

            def hidden_turn(j, e):
                pe.wait_ge(e_hid, EPG * j + e + 1)
                for k in range(4):
                    last = nc.tensor.transpose(B[2 * (e % 2)][:, k * P:k * P + P], hid[:, k * P:k * P + P], ident[:])
                last.then_inc(e_T, 1)

            def expert_down(t, j, e, after=None):
                pe.wait_ge(e_Tlo, EPG * j + e + 1)
                for h in range(HALVES):
                    half(t, h, lambda k, m: hidTh[:, e % 2, k, :], lambda k, m: hidTl[:, e % 2, k, :],
                         [B[4 + h // 2][:, :]], (2 * (h % 2), 2 * (h % 2) + 1), NC, e == 0 and h % 2 == 0,
                         e == EPG - 1 and h % 2 == 1)
                    if after:
                        after(h)

            def scatter(j, c):
                pe.wait_ge(y_lo, 4 * j + c + 1)
                for a in range(NT):
                    n = 2 * c + a
                    pe.wait_ge(y_add, 8 * j + 8 + (n - 1 if n >= 2 else 0))
                    mm(B[2 + a][:, :], selTg[:, a * P:a * P + P], ygh[:, c, :], start=True, stop=False)
                    mm(B[2 + a][:, :], selTg[:, a * P:a * P + P], ygl[:, c, :], start=False, stop=True).then_inc(y_mm, 1)

            def group(t, j, more):
                pe.wait_ge(g_lo, 4 * j + 4)
                expert_up(t, j, 0)
                pe.wait_ge(y_add, 8 * j + 8)
                for e in range(1, EPG):
                    expert_up(t + 3 * e - 1, j, e)
                    if e < EPG - 1:
                        expert_down(t + 3 * e + 1, j, e - 1)

                def after(h):
                    if h == 5:
                        hidden_turn(j, EPG - 1)
                    if more:
                        gather(j + 1, h)
                expert_down(t + T_GROUP - 2, j, EPG - 2, after)

                def after(h):
                    if h == 0:
                        pe.wait_ge(g_table, 2 * j + 2)
                        pe.wait_ge(e_Tlo, EPG * j + EPG)
                    if h in (3, 5, 7):
                        scatter(j, (h - 3) // 2)
                expert_down(t + T_GROUP - 1, j, EPG - 1, after)
                scatter(j, 3)

            for n in range(8):
                gather(0, n)
            with pe.Fori(0, GROUPS - 1) as g:
                group(T_MOE + T_GROUP * g, g, True)
            group(T_OVER - T_GROUP, GROUPS - 1, True)
            over = pe.value_load(flag[0:1, 0:1], min_val=0, max_val=1)
            with pe.If(over > 0):
                group(T_OVER, GROUPS, False)

        @block.scalar
        def _(ac):
            link = Link(ac, act)
            fn = nc.scalar.activation

            def split(t, h0=0, h1=HALVES, width=NC, before=None):
                for h in range(h0, h1):
                    if before:
                        before(h)
                    if h % 2 == 0:
                        ac.wait_ge(landed[h // 2], 16 * (t + 1))
                    ac.wait_ge(slot_free, HALVES * t + h + 1)
                    fn(WH[:, h % 4, :, 0:width], W32[:, h // 2, 2 * (h % 2):2 * (h % 2) + 2, 0:width],
                       ACT.Copy).then_inc(hi_ready, 1)

            def product(t):
                ac.wait_ge(slot_free, SLOT_CREDIT + HALVES * (t + 1))

            def four(b):
                return B[b][:, :].rearrange("p (k n) -> p k n", k=4)

            def turned(g0, dst, r, parts, bank=None):
                a, k4 = r // 4, r % 4
                n = r if bank is None else bank
                ac.wait_ge(tp_ready, g0 + n + 1)
                fn(dst(4 * k4, a), four(4 + n % 2), ACT.Copy).then_inc(tp_hi if parts else tp_free[n % 2], 1)

            ac.dma_start(wif[:], w_in[0].rearrange("(t p) n -> p t n", p=P)[:, :, C_IF:C_IF + 16]).then_inc(if_in, 16)
            ac.dma_start(wukv[:], w_ukv[0].rearrange("(k p) n -> p k n", p=P)).then_inc(small_in, 16)
            ac.dma_start(kvg[:], kv_norm[0:1, :].to_broadcast([P, RANK])).then_inc(small_in, 16)
            ac.dma_start(bif[:, 0:8], m_i_bias[0:1, :].to_broadcast([P, MH])).then_inc(small_in, 16)
            ac.dma_start(bif[:, 8:16], m_f_bias[0:1, :].to_broadcast([P, MH])).then_inc(small_in, 16)
            ac.dma_start(brt[:, 0:4], b_grp[0:1, :].to_broadcast([P, 4])).then_inc(small_in, 16)
            ac.dma_start(brt[:, 4:20], b_exp[0:1, :].to_broadcast([P, NE])).then_inc(small_in, 16)

            for r in range(8):
                turned(G_X, lambda k, a: xTh[:, k:k + 4, a * P:a * P + P], r, True)
            split(T_IDX)
            split(T_IDX + 1)
            split(T_IDX + 2, width=IDX_W - 2 * NC)

            def idx_copy(n):
                a, r = n // 2, n % 2
                ac.wait_ge(idx_T, n + 1)
                if n < 4:
                    fn(iqT[:, 4 * r:4 * r + 4, a * P:a * P + P], four(4 + r), ACT.Copy).then_inc(idx_Tc, 1)
                else:
                    fn(ikT[:], B[6][:, 0:TOK], ACT.Copy).then_inc(idx_Tc, 1)

            def relu(n):
                w = P * (n // 8 + 1)
                ac.wait_ge(sc_mm, n + 1)
                if n >= 2:
                    ac.wait_ge(sc_used, 2 * (n - 1))
                for r in range(2):
                    last = fn(RL[:, n % 2, r * w:r * w + w], B[4 + 2 * (n % 2) + r][:, 0:w], ACT.Relu, scale=ID ** -0.5)
                last.then_inc(sc_relu, 1)

            split(T_MQ)

            def before(h):
                if h < 4:
                    idx_copy(h)
                if h == 4:
                    idx_copy(4)
                    ac.wait_ge(kv_T, 1)
                    fn(kvT[:], B[7][:, :].rearrange("p (k n) -> p k n", k=2), ACT.Copy).then_inc(kv_Tc, 1)
                if h == 6:
                    ac.wait_ge(kv_mm, 1)
                    fn(kT[:], B[6][:, 0:TOK], ACT.Copy).then_inc(kv_c, 1)
                    fn(V[:], B[7][:, 0:TOK].rearrange("p (a n) -> p a n", a=2), ACT.Copy).then_inc(kv_c, 1)
            split(T_MQ + 1, before=before)
            split(T_MQ + 2, before=lambda h: relu(h))
            split(T_MQ + 3, before=lambda h: relu(8 + h))

            def before(h):
                if h == 5:
                    ac.wait_ge(if_in, 16)
                    fn(wifh[:], wif[:], ACT.Copy).then_inc(if_hi, 1)
            split(T_Q, before=before)

            def mq_turned(r):
                turned(G_MQ, lambda k, a: (mqT if k < 8 else mkT)[:, k % 8:k % 8 + 4, a * P:a * P + P], r, False)
            split(T_Q + 1, before=lambda h: mq_turned(h - 4) if h >= 4 else None)
            split(T_Q + 2, before=lambda h: mq_turned(h + 4) if h < 4 else None)

            def before(h):
                if h == 2:
                    ac.wait_ge(row_dve, 1)
                    link(fn(rows[0:MH, 3, :], rows[0:MH, 2, :], ACT.Exp, scale=-1.0))
                    fn(rows[0:MH, 4, :], rows[0:MH, 3, :], ACT.Ln, bias=1.0).then_inc(row_act, 1)
                if h == 6:
                    ac.wait_ge(row_dve, 3)
                    fn(rows[0:MH, 11, :], rows[0:MH, 10, :], ACT.Exp, scale=-1.0).then_inc(row_dve, 1)
            split(T_Q + 3, before=before)
            split(T_MV)

            def q_turned(r):
                turned(G_Q, lambda k, a: aqT[:, k:k + 4, a * P:a * P + P], r, False)
            split(T_MV + 1, before=lambda h: q_turned(h - 4) if h >= 4 else None)

            def exps(b, n0):
                a = b // 2
                ac.wait_ge(lg_max, b + 1)
                for h in range(n0, n0 + 4):
                    fn(LG[:, h, 0:P * (a + 1)], LG[:, h, 0:P * (a + 1)], ACT.Exp, bias=mx[:, h:h + 1],
                       accum_out=rs[:, h:h + 1]).then_inc(lg_exp, 1)

            def probs_copy(b, st):
                ev = (0, 2, 4, 8)[b] + 2 * st
                for q4 in range(2):
                    ac.wait_ge(pt_T, ev + q4 + 1)
                    fn(PT[:, st, q4 * NC:q4 * NC + NC], B[6 + q4][:, :], ACT.Copy).then_inc(pt_c, 1)

            def values_hi(b, q4):
                ac.wait_ge(pv_mm, 2 * b + q4 + 1)
                k = 8 * (b % 2) + 4 * q4
                a = b // 2
                fn(yaTh[:, k:k + 4, a * P:a * P + P], four(6 + q4), ACT.Copy).then_inc(pv_hi, 1)

            def o_gate(j):
                product(T_MO + j)
                b = 2 * ((T_MO + j) % 2)
                for a in range(NT):
                    last = fn(YM[:, a, j * NC:j * NC + NC], B[b + a][:, :], ACT.Sigmoid)
                last.then_inc(bank_free[(T_MO + j) % 2], 1)

            def attend(b):
                def before(h):
                    if h < 4 and b == 0:
                        q_turned(h + 4)
                    if b and h == 0:
                        probs_copy(b - 1, 0)
                    if b > 2 and h == 1:
                        probs_copy(b - 1, 1)
                    if b and h in (2, 3):
                        values_hi(b - 1, h - 2)
                    if b < 4 and h in (5, 6):
                        exps(b, 4 * (h - 5))
                    if b == 3 and h == 7:
                        o_gate(0)
                return before

            split(T_MV + 2, before=attend(0))
            split(T_MV + 3, before=attend(1))
            split(T_MO, before=attend(2))
            split(T_MO + 1, before=attend(3))

            def head_exp(h):
                ac.wait_ge(ml_x, h + 1)
                fn(ex[:], ex[:], ACT.Exp).then_inc(ml_exp, 1)

            def recurrent(first, j):
                def before(h):
                    n = first + h
                    if n >= 4 and n % 2 == 0 and (n - 4) // 2 < MH:
                        head_exp((n - 4) // 2)
                    if h == 3:
                        o_gate(j)
                    if first < 0:
                        attend(4)(h)
                return before
            split(T_MO + 2, before=recurrent(-2, 1))
            split(T_MO + 3, before=recurrent(6, 2))
            split(T_MIX, before=recurrent(14, 3))

            def gate_sig(i, j):
                t = T_MIX + 4 * i + 2 * j
                product(t)
                if i:
                    ac.wait_ge(mix_a if j == 0 else mix_ready, i)
                for a in range(NT):
                    last = fn(sg[:, j, a, :], B[2 * (t % 2) + a][:, :], ACT.Sigmoid)
                last.then_inc(bank_free[t % 2], 1)

            def ym_turned(r):
                turned(G_YM, lambda k, a: ymTh[:, k:k + 4, a * P:a * P + P], r, True)

            order = (0, 4, 1, 5, 2, 6, 3, 7)

            def mix_turned(n):
                turned(G_MIX, lambda k, a: mixTh[:, k:k + 4, a * P:a * P + P], order[n], True, n)

            def before(h):
                if h == 0:
                    ac.wait_ge(ml_out, MH)
                if h == 3:
                    gate_sig(0, 0)
            split(T_MIX + 1, before=before)
            split(T_MIX + 2, before=lambda h: ym_turned(h - 4) if h >= 4 else None)

            def before(h):
                if h < 4:
                    ym_turned(h + 4)
                if h == 3:
                    gate_sig(0, 1)
            split(T_MIX + 3, before=before)
            for i in range(1, 4):
                split(T_MIX + 4 * i)
                split(T_MIX + 4 * i + 1, before=lambda h: gate_sig(i, 0) if h == 3 else None)
                split(T_MIX + 4 * i + 2)

                def before(h):
                    if h == 3:
                        gate_sig(i, 1)
                    if i == 3 and h >= 5:
                        mix_turned(h - 5)
                split(T_MIX + 4 * i + 3, before=before)

            def before(h):
                if h < 3:
                    mix_turned(h + 3)
                if h == 4:
                    product(T_MIX + 15)
                    ac.dma_start(RES[:], x[0].rearrange("(a p) k -> p a k", p=P)).then_inc(x2_in, 16)
                    ac.dma_start(lng[:], ln1_g[0:1, :].to_broadcast([P, D])).then_inc(ln_in, 16)
                    ac.dma_start(lnb[:], ln1_b[0:1, :].to_broadcast([P, D])).then_inc(ln_in, 16)
                    ac.dma_start(wple[:], w_ple[0].rearrange("(k p) n -> p k n", p=P)).then_inc(ple_in, 16)
                if h == 7:
                    mix_turned(6)
            split(T_OUT, before=before)

            def before(h):
                if h == 0:
                    mix_turned(7)
                if h == 1:
                    ac.wait_ge(mix_ready, 4)
                    ac.dma_start(pin[:], p[0, 0].rearrange("(a p) k -> p a k", p=P)).then_inc(ple_in, 16)
            split(T_OUT + 1, before=before)
            split(T_OUT + 2)

            def before(h):
                if h == 4:
                    ac.wait_ge(pT_mm, 1)
                    fn(pT[:], B[6][:, :].rearrange("p (k n) -> p k n", k=2), ACT.Copy).then_inc(pT_c, 1)
            split(T_OUT + 3, before=before)
            product(T_OUT + 3)
            ac.dma_start(wr[:, :, 0:4], w_grp[0].rearrange("(p t) n -> p t n", p=P)).then_inc(r_in, 16)
            ac.dma_start(wr[:, :, 4:20], w_exp[0].rearrange("(p t) n -> p t n", p=P)).then_inc(r_in, 16)

            def pp_copy(n):
                ac.wait_ge(pp_mm, n + 1)
                fn(pp[:, n // 4, n % 4 * NC:n % 4 * NC + NC], B[4 + n % 4][:, :], ACT.Copy).then_inc(pp_c, 1)

            def scaled(n, k):
                a, c = k // 4, slice(k % 4 * NC, k % 4 * NC + NC)
                fn(RES[:, a, c], RES[:, a, c], ACT.Identity, bias=nmr[:, a:a + 1], scale=rstd[:, a:a + 1]).then_inc(nrm_a, 1)

            for n in range(4):
                pp_copy(n)
            ac.wait_ge(nmr_ready, 1)
            for k in range(8):
                scaled(1, k)
                if k % 2:
                    pp_copy(4 + k // 2)
            for a in range(NT):
                ac.wait_ge(nrm_b, 4 * a + 4)
                fn(h1h[:, a, :, :].rearrange("p t q -> p q t"), RES[:, a, :].rearrange("p (q t) -> p q t", t=KT),
                   ACT.Copy).then_inc(h1_hi, 1)
                if a == 0:
                    ac.wait_ge(r_in, 32)
                    fn(wrh[:], wr[:], ACT.Copy).then_inc(r_hi, 1)

            split(T_PLE, 0, 3)
            for n in range(8):
                a, k4 = n // 4, n % 4
                ac.wait_ge(hT_mm, n + 1)
                fn(hTh[:, 4 * k4:4 * k4 + 4, a * P:a * P + P], four(4 + n % 2), ACT.Copy).then_inc(hT_hi, 1)
            split(T_PLE, 3)

            def ple_gate(j):
                product(T_PLE + j)
                if j:
                    ac.wait_ge(ple_done, j)
                for a in range(NT):
                    last = fn(psg[:, a, :], B[2 * ((T_PLE + j) % 2) + a][:, :], ACT.Sigmoid)
                last.then_inc(bank_free[(T_PLE + j) % 2], 1)

            def before(h):
                if h == 3:
                    ple_gate(0)
                if h == 4:
                    ac.wait_ge(r_one, 1)
                    fn(r2[:, 0:8], r1[:, 0:8], ACT.Exp).then_inc(r_exp, 1)
            split(T_PLE + 1, before=before)

            def before(h):
                if h == 3:
                    ple_gate(1)
                if h == 1:
                    ac.wait_ge(r_log, 1)
                    fn(r4[:, 0:8], r3[:, 0:8], ACT.Exp).then_inc(r_exp, 1)
            split(T_PLE + 2, before=before)
            split(T_PLE + 3, before=lambda h: ple_gate(2) if h == 3 else None)
            split(T_MOE, 0, 3)
            ple_gate(3)
            ac.dma_start(ln2g[:], ln2_g[0:1, :].to_broadcast([P, D])).then_inc(ln2_in, 16)
            ac.dma_start(ln2b[:], ln2_b[0:1, :].to_broadcast([P, D])).then_inc(ln2_in, 16)

            def gathered(j, n):
                ac.wait_ge(g_mm, 8 * j + n + 1)
                fn(xgh[:, 4 * n:4 * n + 4, :], four(n % 2), ACT.Copy).then_inc(g_hi, 1)

            def group(t, j, more, last):
                def sig(e):
                    product(t + (3 * e if e else 1))
                    ac.wait_ge(e_link, EPG * j + e + 1)
                    fn(sgm[:], B[2 * (e % 2)][:, :], ACT.Sigmoid).then_inc(e_sig, 1)

                def hidden_hi(e):
                    ac.wait_ge(e_T, EPG * j + e + 1)
                    fn(hidTh[:, e % 2, :, :], four(2 * (e % 2)), ACT.Copy).then_inc(e_Thi, 1)

                def y_part(c):
                    ac.wait_ge(slot_free, SLOT_CREDIT + HALVES * (t + T_GROUP - 1) + 2 * c + 2)
                    fn(ygh[:, c, :], B[4 + c][:, :], ACT.Copy).then_inc(y_hi, 1)

                split(t, 3)
                split(t + 1)
                for e in range(1, EPG):
                    split(t + 3 * e - 1, before=lambda h: sig(e - 1) if h == 3 else None)
                    split(t + 3 * e, before=lambda h: hidden_hi(e - 1) if h == 3 else None)
                    if e < EPG - 1:
                        split(t + 3 * e + 1)

                def before(h):
                    if h == 3:
                        sig(EPG - 1)
                    if more and h >= 4:
                        gathered(j + 1, h - 4)
                split(t + T_GROUP - 2, before=before)

                def before(h):
                    if h == 1:
                        hidden_hi(EPG - 1)
                    if h == 6:
                        y_part(0)
                split(t + T_GROUP - 1, before=before)
                y_part(1)
                if last:
                    y_part(2)
                    y_part(3)
                else:
                    split(t + T_GROUP, 0, 1)
                    y_part(2)
                    split(t + T_GROUP, 1, 3)
                    y_part(3)

            ac.wait_ge(ple_done, 4)
            for n in range(4):
                gathered(0, n)
            with ac.Fori(0, GROUPS - 1) as g:
                group(T_MOE + T_GROUP * g, g, True, False)
            group(T_OVER - T_GROUP, GROUPS - 1, True, True)
            over = ac.value_load(flag[0:1, 0:1], min_val=0, max_val=1)
            with ac.If(over > 0):
                split(T_OVER, 0, 3)
                group(T_OVER, GROUPS, False, True)
            ac.wait_ge(nmr_ready, 2)
            for k in range(8):
                scaled(2, k)

        @block.vector
        def _(dv):
            link = Link(dv, dve)
            v = nc.vector
            stt = nc.vector.scalar_tensor_tensor

            def split(t, h0=0, h1=HALVES, width=NC, before=None):
                for h in range(h0, h1):
                    if before:
                        before(h)
                    dv.wait_ge(hi_ready, HALVES * t + h + 1)
                    v.tensor_tensor(WL[:, h % 4, :, 0:width], W32[:, h // 2, 2 * (h % 2):2 * (h % 2) + 2, 0:width],
                                    WH[:, h % 4, :, 0:width].bitcast(F32), ALU.subtract).then_inc(lo_ready, 1)

            def product(t):
                dv.wait_ge(slot_free, SLOT_CREDIT + HALVES * (t + 1))

            def four(b):
                return B[b][:, :].rearrange("p (k n) -> p k n", k=4)

            def turned(h0, hi, lo, r, n):
                a, k4 = r // 4, r % 4
                dv.wait_ge(tp_hi, h0 + n + 1)
                s = (slice(None), slice(4 * k4, 4 * k4 + 4), slice(a * P, a * P + P))
                v.tensor_tensor(lo[s], four(4 + n % 2), hi[s].bitcast(F32), ALU.subtract).then_inc(tp_free[n % 2], 1)

            def evac(t, dst):
                product(t)
                for a in range(NT):
                    w = dst(a).shape[-1] if len(dst(a).shape) == 2 else NC
                    src = B[2 * (t % 2) + a][:, 0:w]
                    if len(dst(a).shape) == 3:
                        src = src.rearrange("p (h n) -> p h n", n=dst(a).shape[-1])
                    last = v.tensor_copy(dst(a), src)
                last.then_inc(bank_free[t % 2], 1)

            def at_three(f, *args):
                return lambda h: f(*args) if h == 3 else None

            dv.sem_inc(lo_ready, RING_CREDIT)
            dv.sem_inc(y_add, 8)
            dv.sem_inc(e_link, 1)
            for r in range(8):
                turned(0, xTh, xTl, r, r)

            def idx_rows(j):
                w = min(NC, IDX_W - NC * j)
                evac(T_IDX + j, lambda a: P1[:, a, NC * j:NC * j + w])

            split(T_IDX)
            split(T_IDX + 1, before=at_three(idx_rows, 0))
            split(T_IDX + 2, width=IDX_W - 2 * NC, before=at_three(idx_rows, 1))

            def before(h):
                if h == 3:
                    idx_rows(2)
                    dv.wait_ge(bank_free[0], 3)
                    dv.wait_ge(bank_free[1], 2)
                    v.tensor_copy(P1[:, :, 1360:1424], P1[:, :, 1280:1344]).then_inc(idx_evac, 1)
                    v.tensor_copy(P1[:, :, 1424:1488], P1[:, :, 1280:1344]).then_inc(idx_evac, 1)
                    v.tensor_scalar(iw4.rearrange("p (a h) -> p a h", a=2), P1[:, :, 1344:1360], IH ** -0.5, None,
                                    ALU.mult).then_inc(idx_evac, 1)
                if h == 4:
                    for a in range(NT):
                        link(stt(out=kvn[:, a, :], in0=P1[:, a, 0:RANK], scalar=1.0, in1=P1[:, a, 0:RANK], op0=ALU.mult,
                                 op1=ALU.mult, accum_out=rstd[:, a:a + 1]))
                    dv.wait_ge(const_ready, 1)
                    v.tensor_scalar(rstd, rstd, 1.0 / RANK, EPS, ALU.mult, ALU.add).then_inc(rms_ss, 1)
                    v.tensor_copy(identR[:], ident[:]).then_inc(identr_ready, 1)
                    v.memset(SC[:], 0.0).then_inc(idx_evac, 1)
                if h == 6:
                    dv.wait_ge(rms_r, 1)
                    dv.wait_ge(small_in, 96)
                    for a in range(NT):
                        ins = stt(out=kvn[:, a, :], in0=P1[:, a, 0:RANK], scalar=rstd[:, a:a + 1], in1=kvg[:],
                                  op0=ALU.mult, op1=ALU.mult)
                    ins.then_inc(kvn_ready, 1)
                    dv.wait_ge(idx_evac, 4)
            split(T_MQ, before=before)

            def score_sum(n):
                a, j, w = n // 8, n % 8, P * (n // 8 + 1)
                dv.wait_ge(sc_relu, n + 1)
                for r in range(2):
                    h = 16 * a + 2 * j + r
                    dv.wait_ge(sc_used, 2 * n + r) if 2 * n + r else None
                    stt(out=SC[:, a, 0:w], in0=RL[:, n % 2, r * w:r * w + w], scalar=iw4[:, h:h + 1],
                        in1=SC[:, a, 0:w], op0=ALU.mult, op1=ALU.add).then_inc(sc_used, 1)

            def mq_rows(j):
                evac(T_MQ + j, lambda a: tokm[:, a, NC * j:NC * j + NC])

            def before(h):
                if h == 3:
                    mq_rows(0)
            split(T_MQ + 1, before=before)

            def before(h):
                if h == 3:
                    mq_rows(1)
                score_sum(h)
            split(T_MQ + 2, before=before)

            def before(h):
                if h == 3:
                    mq_rows(2)
                score_sum(8 + h)
            split(T_MQ + 3, before=before)

            def best(n):
                a = n // 8
                if n % 8 == 0:
                    dv.wait_ge(sc_masked, a + 1)
                sc = SC[:, a, 0:P * (a + 1)]
                link(v.max(m8, sc))
                link(v.match_replace(sc, m8, sc, TAKEN))

            def chosen():
                for a in range(NT):
                    w = P * (a + 1)
                    link(v.tensor_scalar(MK[:, a, 0:w], SC[:, a, 0:w], TAKEN, None, ALU.is_equal))
                    last = v.tensor_scalar(MK[:, a, 0:w], MK[:, a, 0:w], -NEG, NEG, ALU.mult, ALU.add)
                last.then_inc(topk_done, 1)

            def before(h):
                if h == 3:
                    mq_rows(3)
                if h >= 2:
                    best(h - 2)
                if h == 7:
                    dv.wait_ge(if_hi, 1)
                    v.tensor_tensor(wifl[:], wif[:], wifh[:].bitcast(F32), ALU.subtract).then_inc(if_lo, 1)
            split(T_Q, before=before)

            def q_rows(j):
                evac(T_Q + j, lambda a: tokq[:, a, NC * j:NC * j + NC])

            def before(h):
                if h == 3:
                    q_rows(0)
                best(6 + h)
            split(T_Q + 1, before=before)

            R = [rows[0:MH, r, :] for r in range(13)]

            def before(h):
                if h < 2:
                    best(14 + h)
                if h == 2:
                    chosen()
                if h == 3:
                    q_rows(1)
                if h == 5:
                    dv.wait_ge(if_mm, 2)
                    v.tensor_tensor(ift.rearrange("p (a n) -> p a n", a=2), B[6][:, 0:32].rearrange("p (a n) -> p a n", a=2),
                                    bif.unsqueeze(1).to_broadcast([P, 2, 16]), ALU.add).then_inc(if_tok, 1)
            split(T_Q + 2, before=before)

            def before(h):
                if h == 0:
                    dv.wait_ge(if_T, 1)
                    dv.wait_ge(tp_free[0], G_Q // 2)
                    dv.wait_ge(tp_free[1], G_Q // 2)
                    link(v.tensor_copy(R[0], B[7][0:MH, 0:TOK]))
                    link(v.tensor_copy(R[1], B[7][0:MH, TOK:2 * TOK]))
                    link(v.memset(R[12], 1.0))
                    stt(out=R[2], in0=R[1], scalar=-1.0, in1=R[1], op0=ALU.mult, op1=ALU.max).then_inc(row_dve, 1)
                if h == 3:
                    q_rows(2)
                if h == 4:
                    dv.wait_ge(row_act, 1)
                    link(stt(out=R[5], in0=R[1], scalar=0.0, in1=R[4], op0=ALU.min, op1=ALU.subtract))
                    link(v.tensor_tensor_scan(R[6], R[12], R[5], 0.0, ALU.mult, ALU.add))
                if h == 5:
                    link(v.tensor_tensor(R[7], R[0], R[6], ALU.subtract))
                    link(v.tensor_tensor_scan(R[8], R[7], R[7], 0.0, ALU.max, ALU.max))
                    v.tensor_scalar(negG[0:MH, :], R[8], -1.0, None, ALU.mult).then_inc(row_dve, 1)
                    v.tensor_tensor(R[10], R[6], R[8], ALU.add).then_inc(row_dve, 1)
            split(T_Q + 3, before=before)

            def before(h):
                if h == 2:
                    dv.wait_ge(row_T, 1)
                    link(v.tensor_copy(ut, B[6][:, 0:16]))
                    v.tensor_copy(en, B[6][:, 16:32]).then_inc(row_Tc, 1)
                if h == 3:
                    q_rows(3)
            split(T_MV, before=before)

            def mv_rows(j):
                evac(T_MV + j, lambda a: mv[:, a, 2 * j:2 * j + 2, 0:MV])

            def before(h):
                if h == 3:
                    link(v.memset(mv[:, :, :, MV:MV + 1], 1.0))
                    mv_rows(0)
            split(T_MV + 1, before=before)

            def read_logits(b, j):
                n, w = 4 * b + j, P * (b // 2 + 1)
                if j == 0:
                    dv.wait_ge(lg_bias, b + 1)
                dv.wait_ge(lg_mm, n + 1)
                stt(out=LG[:, 2 * j:2 * j + 2, 0:w], in0=B[4 + n % 2][:, 0:2 * w].rearrange("p (h n) -> p h n", h=2),
                    scalar=DH ** -0.5, in1=LG[:, 2 * j:2 * j + 2, 0:w], op0=ALU.mult, op1=ALU.add).then_inc(lg_read, 1)

            def values_lo(b, q4):
                dv.wait_ge(pv_hi, 2 * b + q4 + 1)
                k, a = 8 * (b % 2) + 4 * q4, b // 2
                s = (slice(None), slice(k, k + 4), slice(a * P, a * P + P))
                v.tensor_tensor(yaTl[s], four(6 + q4), yaTh[s].bitcast(F32), ALU.subtract).then_inc(pv_lo, 1)

            def attend(b, rows_of):
                def before(h):
                    if b and h in (2, 3):
                        values_lo(b - 1, h - 2)
                    if h == 3 and rows_of is not None:
                        mv_rows(rows_of)
                    if b == 4:
                        return
                    w = P * (b // 2 + 1)
                    if h in (4, 5):
                        read_logits(b, 2 * (h - 4))
                        read_logits(b, 2 * (h - 4) + 1)
                    if h == 5:
                        dv.wait_ge(lg_read, 4 * b + 4)
                        v.tensor_reduce(mx, LG[:, :, 0:w], AX, ALU.max, negate=True).then_inc(lg_max, 1)
                    if h == 7:
                        dv.wait_ge(lg_exp, 8 * b + 8)
                        link(v.reciprocal(ri, rs))
                        v.tensor_tensor(LG[:, :, 0:w], LG[:, :, 0:w], ri.unsqueeze(2).to_broadcast([P, 8, w]),
                                        ALU.mult).then_inc(pr_norm, 1)
                return before

            split(T_MV + 2, before=attend(0, 1))
            split(T_MV + 3, before=attend(1, 2))
            split(T_MO, before=attend(2, 3))
            split(T_MO + 1, before=attend(3, None))

            def head_exponents(h):
                dv.wait_ge(ml_qk, h + 1)
                stt(out=ex[:, 0:TOK], in0=B[4][:, 0:TOK], scalar=ut[:, h:h + 1], in1=CM[:], op0=ALU.add, op1=ALU.add)
                stt(out=ex[:, TOK:384], in0=B[4][:, P:TOK], scalar=ut[:, 8 + h:9 + h], in1=CM[:, 0:P], op0=ALU.add,
                    op1=ALU.add).then_inc(ml_x, 1)

            def head_weights(h):
                dv.wait_ge(ml_exp, h + 1)
                if h:
                    dv.wait_ge(ml_num, h)
                stt(out=wt[:], in0=B[5][:, 0:384], scalar=MQ ** -0.5, in1=ex[:], op0=ALU.mult, op1=ALU.mult).then_inc(ml_w, 1)

            def head_out(h):
                dv.wait_ge(ml_num, h + 1)
                for a in range(NT):
                    b = B[6 + a]
                    link(stt(out=dn[:, a:a + 1], in0=b[:, MV:MV + 1], scalar=-1.0, in1=en[:, 8 * a + h:8 * a + h + 1],
                             op0=ALU.mult, op1=ALU.max))
                    link(v.tensor_tensor(dn[:, a:a + 1], dn[:, a:a + 1], b[:, MV:MV + 1], ALU.max))
                link(v.reciprocal(rdn, dn))
                t = T_MO + h // 2
                dv.wait_ge(bank_free[t % 2], t // 2 + 2)
                for a in range(NT):
                    ym = YM[:, a, h * MV:h * MV + MV]
                    last = stt(out=ym, in0=B[6 + a][:, 0:MV], scalar=rdn[:, a:a + 1], in1=ym, op0=ALU.mult, op1=ALU.mult)
                last.then_inc(ml_out, 1)

            def recurrent(first):
                def before(h):
                    n = first + h
                    if first < 0:
                        attend(4, None)(h)
                    if n >= 4 and n % 2 == 0 and (n - 4) // 2 < MH:
                        head_exponents((n - 4) // 2)
                    if n >= 7 and n % 2 == 1 and (n - 7) // 2 < MH:
                        head_out((n - 7) // 2)
                    if n >= 5 and n % 2 == 1 and (n - 5) // 2 < MH:
                        head_weights((n - 5) // 2)
                return before
            split(T_MO + 2, before=recurrent(-2))
            split(T_MO + 3, before=recurrent(6))
            split(T_MIX, before=recurrent(14))

            def mix_part(i, j):
                t = T_MIX + 4 * i + 2 * j + 1
                product(t)
                dv.wait_ge(bank_free[(t - 1) % 2], (t - 1) // 2 + 2)
                for a in range(NT):
                    src, m = B[2 * (t % 2) + a][:, :], MIX[:, a, NC * i:NC * i + NC]
                    last = v.tensor_tensor(sg[:, 1, a, :] if j else m, src, sg[:, j, a, :], ALU.mult)
                last.then_inc(bank_free[t % 2], 1)
                if j == 0:
                    dv.wait_ge(bank_free[t % 2], t // 2 + 2)
                    dv.sem_inc(mix_a, 1)
                else:
                    dv.wait_ge(bank_free[t % 2], t // 2 + 2)
                    v.tensor_tensor(MIX[:, :, NC * i:NC * i + NC], MIX[:, :, NC * i:NC * i + NC], sg[:, 1, :, :],
                                    ALU.add).then_inc(mix_ready, 1)

            def before(h):
                n = 22 + h
                if n - 7 < 16 and n % 2 == 1:
                    head_out((n - 7) // 2)
            split(T_MIX + 1, before=before)

            def before(h):
                if h == 3:
                    mix_part(0, 0)
                if h >= 4:
                    turned(8, ymTh, ymTl, h - 4, h - 4)
            split(T_MIX + 2, before=before)
            split(T_MIX + 3, before=lambda h: turned(8, ymTh, ymTl, h + 4, h + 4) if h < 4 else None)
            order = (0, 4, 1, 5, 2, 6, 3, 7)

            def mix_turned(n):
                turned(16, mixTh, mixTl, order[n], n)

            for i in range(1, 4):
                split(T_MIX + 4 * i, before=at_three(mix_part, i - 1, 1))
                split(T_MIX + 4 * i + 1)
                split(T_MIX + 4 * i + 2, before=at_three(mix_part, i, 0))
                split(T_MIX + 4 * i + 3, before=lambda h: mix_turned(h - 5) if i == 3 and h >= 5 else None)

            def res_part(j):
                t = T_OUT + j
                product(t)
                if j == 0:
                    dv.wait_ge(x2_in, 16)
                for a in range(NT):
                    r = RES[:, a, NC * j:NC * j + NC]
                    last = stt(out=r, in0=r, scalar=ALPHA, in1=B[2 * (t % 2) + a][:, :], op0=ALU.mult, op1=ALU.add)
                last.then_inc(bank_free[t % 2], 1)
                dv.wait_ge(bank_free[t % 2], t // 2 + 2)
                for a in range(NT):
                    link(v.bn_stats(bnst[:, 24 * a + 6 * j:24 * a + 6 * j + 6], RES[:, a, NC * j:NC * j + NC]))

            def before(h):
                if h < 3:
                    mix_turned(h + 3)
                if h == 3:
                    mix_part(3, 1)
                if h == 7:
                    mix_turned(6)
            split(T_OUT, before=before)

            def before(h):
                if h == 0:
                    mix_turned(7)
                if h == 3:
                    res_part(0)
            split(T_OUT + 1, before=before)
            split(T_OUT + 2, before=at_three(res_part, 1))
            split(T_OUT + 3, before=at_three(res_part, 2))
            res_part(3)

            def norm(n, gr, ready):
                for a in range(NT):
                    link(v.bn_aggr(mv2[:, 2 * a:2 * a + 2], bnst[:, 24 * a:24 * a + 24]))
                mean, var = (mv2.rearrange("p (a n) -> p a n", n=2)[:, :, k] for k in range(2))
                v.tensor_scalar(rstd, var, EPS, None, ALU.add).then_inc(var_ready, 1)
                dv.wait_ge(rstd_ready, n)
                stt(out=nmr, in0=mean, scalar=-1.0, in1=rstd, op0=ALU.mult, op1=ALU.mult).then_inc(nmr_ready, 1)
                dv.wait_ge(ready, 32)
                for k in range(8):
                    a, c = k // 4, slice(k % 4 * NC, k % 4 * NC + NC)
                    dv.wait_ge(nrm_a, 8 * (n - 1) + k + 1)
                    v.tensor_tensor(RES[:, a, c], RES[:, a, c], gr[:, c], ALU.mult).then_inc(nrm_g, 1)

            norm(1, lng, ln_in)
            for a in range(NT):
                dv.wait_ge(h1_hi, a + 1)
                v.tensor_tensor(h1l[:, a, :, :].rearrange("p t q -> p q t"), RES[:, a, :].rearrange("p (q t) -> p q t", t=KT),
                                h1h[:, a, :, :].rearrange("p t q -> p q t").bitcast(F32), ALU.subtract).then_inc(h1_lo, 1)
                if a == 0:
                    dv.wait_ge(r_hi, 1)
                    v.tensor_tensor(wrl[:], wr[:], wrh[:].bitcast(F32), ALU.subtract).then_inc(r_lo, 1)
            split(T_PLE, 0, 3)
            for n in range(8):
                a, k4 = n // 4, n % 4
                dv.wait_ge(hT_mml, n + 1)
                v.tensor_copy(hTl[:, 4 * k4:4 * k4 + 4, a * P:a * P + P], four(6 + n % 2)).then_inc(hT_lo, 1)

            def two(ap):
                return ap.rearrange("p (a n) -> p a n", a=2)

            def router_logits():
                dv.wait_ge(r_mm, 2)
                link(v.tensor_tensor(two(lgt), two(B[7][:, 0:40]), brt.unsqueeze(1).to_broadcast([P, 2, 20]), ALU.add))
                link(v.memset(rp, PAD))
                link(v.memset(tk8, PAD))
                link(v.tensor_copy(two(rp)[:, :, 0:4], two(lgt)[:, :, 0:4]))

            def best_group(a):
                link(v.max(m8, rp[:, 16 * a:16 * a + 16]))
                link(v.tensor_copy(tk8[:, 0:1], m8[:, 0:1]))
                link(v.match_replace(r3[:, 16 * a:16 * a + 16], tk8, rp[:, 16 * a:16 * a + 16], TAKEN))
                link(v.tensor_scalar(r1[:, 4 * a:4 * a + 4], lgt[:, 20 * a:20 * a + 4], m8[:, 0:1], None, ALU.subtract))

            def group_one_hot():
                v.tensor_scalar(two(oneh), two(r3)[:, :, 0:4], TAKEN, None, ALU.is_equal).then_inc(r_one, 1)
                dv.wait_ge(r_one, 1)

            def expert_logits(a):
                for g in range(GROUPS):
                    o = r4[:, 8 + 4 * a:12 + 4 * a]
                    lg, w = lgt[:, 20 * a + 4 + 4 * g:20 * a + 8 + 4 * g], oneh[:, 4 * a + g:4 * a + g + 1]
                    if g == 0:
                        link(v.tensor_scalar(o, lg, w, None, ALU.mult))
                    else:
                        link(stt(out=o, in0=lg, scalar=w, in1=o, op0=ALU.mult, op1=ALU.add))

            def group_prob():
                dv.wait_ge(r_exp, 1)
                link(v.tensor_reduce(gp[:, 0:2], two(r2[:, 0:8]), AX, ALU.add))
                link(v.reciprocal(gp[:, 2:4], gp[:, 0:2]))
                link(v.memset(rp, PAD))
                link(v.tensor_copy(two(rp)[:, :, 0:4], two(r4[:, 8:16])))

            def best_experts(a):
                link(v.max(m8, rp[:, 16 * a:16 * a + 16]))
                link(v.tensor_copy(tk8[:, 0:2], m8[:, 0:2]))
                link(v.match_replace(r1[:, 16 * a:16 * a + 16], tk8, rp[:, 16 * a:16 * a + 16], TAKEN))
                link(v.tensor_scalar(r3[:, 4 * a:4 * a + 4], r4[:, 8 + 4 * a:12 + 4 * a], m8[:, 0:1], None, ALU.subtract))

            def experts_one_hot():
                v.tensor_scalar(two(combw), two(r1)[:, :, 0:4], TAKEN, None, ALU.is_equal).then_inc(r_log, 1)

            def combine():
                dv.wait_ge(r_exp, 2)
                link(v.tensor_tensor(combw, r4[:, 0:8], combw, ALU.mult))
                link(v.tensor_reduce(gp[:, 0:2], two(combw), AX, ALU.add))
                link(v.reciprocal(m8[:, 0:2], gp[:, 0:2]))
                link(v.tensor_tensor(gp[:, 0:2], m8[:, 0:2], gp[:, 2:4], ALU.mult))
                for a in range(NT):
                    link(v.tensor_scalar(combw[:, 4 * a:4 * a + 4], combw[:, 4 * a:4 * a + 4], gp[:, a:a + 1], None, ALU.mult))

            def places():
                dv.wait_ge(r_cum, 1)
                link(v.tensor_copy(cum, B[6][:, 0:8]))
                link(v.tensor_copy(tot, B[6][:, 8:12]))
                for a in range(NT):
                    link(v.tensor_tensor(r1[:, 0:4], cum[:, 4 * a:4 * a + 4], oneh[:, 4 * a:4 * a + 4], ALU.mult))
                    link(v.tensor_reduce(pos[:, a:a + 1], r1[:, 0:4], AX, ALU.add))
                link(v.tensor_scalar(pos[:, 2:4], pos[:, 0:2], float(P), None, ALU.is_le))

            def slots(a):
                o = tslot[:, 5 * a:5 * a + 4]
                link(v.tensor_scalar(o, oneh[:, 4 * a:4 * a + 4], pos[:, a:a + 1], pos[:, 2 + a:3 + a], ALU.mult, ALU.mult))
                link(v.tensor_scalar(o, o, -1.0, None, ALU.add))
                link(v.tensor_scalar(tslot[:, 5 * a + 4:5 * a + 5], pos[:, a:a + 1], -float(P) - 1.0, None, ALU.add))

            def select(a):
                dv.wait_ge(iota_ready, 1)
                for j in range(GROUPS + 1):
                    last = v.tensor_scalar(sel[:, a, j, :], iota[:], tslot[:, 5 * a + j:5 * a + j + 1], None, ALU.is_equal)
                link(last) if a == 0 else last.then_inc(r_sel, 1)

            def overflow():
                link(v.tensor_scalar(r1[:, 0:4], tot, float(P), None, ALU.is_gt))
                link(v.tensor_reduce(flagf[:, 0:1], r1[:, 0:4], AX, ALU.add))
                link(v.tensor_tensor(r2[:, 0:4], r1[:, 0:4], iota[:, 0:4], ALU.mult))
                link(v.tensor_reduce(flagf[:, 1:2], r2[:, 0:4], AX, ALU.add))
                link(v.tensor_copy(flag[:], flagf[:, 0:2]))

            def slots_turned(j):
                dv.wait_ge(r_selT, j + 1)
                v.tensor_copy(selT[:, j, :], B[4 + j % 2][:, 0:TOK]).then_inc(r_selTc, 1)

            def ple_part(j):
                t = T_PLE + j
                dv.wait_ge(bank_free[t % 2], t // 2 + 2)
                c = slice(NC * j, NC * j + NC)
                if j == 0:
                    dv.wait_ge(pp_c, 8)
                    dv.wait_ge(h1_scaled, 2)
                link(v.tensor_tensor(psg[:], psg[:], pp[:, :, c], ALU.mult))
                v.tensor_tensor(RES[:, :, c], RES[:, :, c], psg[:], ALU.add).then_inc(ple_done, 1)

            def before(h):
                if h == 5:
                    router_logits()
                if h == 6:
                    best_group(0)
                if h == 7:
                    best_group(1)
            split(T_PLE, 3, before=before)

            def before(h):
                if h == 0:
                    group_one_hot()
                if h in (1, 2):
                    expert_logits(h - 1)
                if h == 4:
                    ple_part(0)
                if h == 5:
                    group_prob()
                if h in (6, 7):
                    best_experts(h - 6)
            split(T_PLE + 1, before=before)

            def before(h):
                if h == 0:
                    experts_one_hot()
                if h == 1:
                    places()
                if h == 2:
                    combine()
                if h == 4:
                    ple_part(1)
                if h == 5:
                    slots(0)
                    slots(1)
                if h in (6, 7):
                    select(h - 6)
            split(T_PLE + 2, before=before)

            def before(h):
                if h == 0:
                    overflow()
                if 2 <= h < 7:
                    slots_turned(h - 2)
                if h == 4:
                    ple_part(2)
                if h == 7:
                    dv.wait_ge(r_cs, 1)
                    v.tensor_copy(cslot[:], B[6][:, 0:20].rearrange("p (j e) -> p j e", e=4)).then_inc(r_all, 1)
            split(T_PLE + 3, before=before)
            split(T_MOE, 0, 3)
            ple_part(3)
            dv.wait_ge(ple_done, 4)

            def gathered(j, n):
                dv.wait_ge(g_mm, 8 * j + 4 + n + 1)
                v.tensor_copy(xgl[:, 4 * n:4 * n + 4, :], four(n % 2)).then_inc(g_lo, 1)

            def group(t, j, more, last):
                def hidden(e):
                    k = EPG * j + e
                    dv.wait_ge(e_sig, k + 1)
                    if e == 0:
                        dv.wait_ge(g_table, 2 * j + 2)
                    stt(out=gcs[:], in0=B[2 * (e % 2)][:, :], scalar=cg[:, e:e + 1], in1=sgm[:], op0=ALU.mult,
                        op1=ALU.mult).then_inc(e_link, 1)
                    dv.wait_ge(e_link, k + 2)
                    if e:
                        dv.wait_ge(e_T, k)
                    v.tensor_tensor(hid[:], gcs[:], B[2 * (e % 2) + 1][:, :], ALU.mult).then_inc(e_hid, 1)

                def hidden_lo(e):
                    dv.wait_ge(e_Thi, EPG * j + e + 1)
                    v.tensor_tensor(hidTl[:, e % 2, :, :], four(2 * (e % 2)), hidTh[:, e % 2, :, :].bitcast(F32),
                                    ALU.subtract).then_inc(e_Tlo, 1)

                def y_part(c):
                    dv.wait_ge(y_hi, 4 * j + c + 1)
                    v.tensor_tensor(ygl[:, c, :], B[4 + c][:, :], ygh[:, c, :].bitcast(F32), ALU.subtract).then_inc(y_lo, 1)

                def add(c):
                    for a in range(NT):
                        dv.wait_ge(y_mm, 8 * j + 2 * c + a + 1)
                        r = RES[:, a, NC * c:NC * c + NC]
                        v.tensor_tensor(r, r, B[2 + a][:, :], ALU.add).then_inc(y_add, 1)

                split(t, 3)
                split(t + 1)
                for e in range(1, EPG):
                    split(t + 3 * e - 1, before=lambda h: hidden(e - 1) if h == 3 else None)
                    split(t + 3 * e, before=lambda h: hidden_lo(e - 1) if h == 3 else None)
                    if e < EPG - 1:
                        split(t + 3 * e + 1)
                split(t + T_GROUP - 2, before=lambda h: hidden(EPG - 1) if h == 3 else None)

                def before(h):
                    if h == 1:
                        hidden_lo(EPG - 1)
                    if more and h < 4:
                        gathered(j + 1, h)
                    if h == 6:
                        y_part(0)
                split(t + T_GROUP - 1, before=before)
                add(0)
                y_part(1)
                if not last:
                    split(t + T_GROUP, 0, 1)
                add(1)
                y_part(2)
                if not last:
                    split(t + T_GROUP, 1, 3)
                y_part(3)
                add(2)
                add(3)

            for n in range(4):
                gathered(0, n)
            with dv.Fori(0, GROUPS - 1) as g:
                group(T_MOE + T_GROUP * g, g, True, False)
            group(T_OVER - T_GROUP, GROUPS - 1, True, True)
            over = dv.value_load(flag[0:1, 0:1], min_val=0, max_val=1)
            dv.wait_ge(y_add, 8 * GROUPS + 8)
            with dv.If(over > 0):
                split(T_OVER, 0, 3)
                group(T_OVER, GROUPS, False, True)
                dv.wait_ge(y_add, 8 * (GROUPS + 1) + 8)
            for a in range(NT):
                for c in range(4):
                    link(v.bn_stats(bnst[:, 24 * a + 6 * c:24 * a + 6 * c + 6], RES[:, a, NC * c:NC * c + NC]))
            norm(2, ln2g, ln2_in)


_INS = ['x', 'p', 'w_in', 'kv_norm', 'w_ukv', 'm_i_bias', 'm_f_bias', 'w_proj_a', 'w_proj_m', 'w_out', 'ln1_g', 'ln1_b',
        'w_grp', 'b_grp', 'w_exp', 'b_exp', 'w_gate', 'w_up', 'w_down', 'w_ple', 'w_ple_gate', 'ln2_g', 'ln2_b']
_OUTS = [((1, 256, 2048), 'float32')]


def kernel(**inputs):
    import numpy as _np
    import concourse.bacc as _bacc
    from concourse import mybir as _mybir
    from concourse.bass_utils import run_bass_kernel_spmd as _run

    nc = _bacc.Bacc("TRN2", target_bir_lowering=False, num_devices=1)
    arrays, args = {}, []
    for name in _INS:
        a = _np.ascontiguousarray(inputs[name])
        arrays[f"in_{name}_dram"] = a
        args.append(nc.dram_tensor(f"in_{name}_dram", a.shape, _mybir.dt.from_np(a.dtype), kind="ExternalInput").ap())
    for i, (shape, dtype) in enumerate(_OUTS):
        dt = _mybir.dt.from_np(_np.dtype(dtype))
        args.append(nc.dram_tensor(f"out_{i}_dram", shape, dt, kind="ExternalOutput").ap())
    build(nc, *args)
    r = _run(nc, [arrays], core_ids=[0])
    return r.results[0]["out_0_dram"]
```
